# Optimizing a Trainium2 kernel written in Bass

```python
import math
import jax
import jax.numpy as jnp
from jax import lax
import numpy as np

D_MODEL = 1024
BATCH = 1
SEQ = 256
DEPTH = 2

ATT_HEADS = 4
ATT_HEAD_DIM = 64
ATT_WIDTH = ATT_HEADS * ATT_HEAD_DIM
DILATED_PATTERNS = ((128, 1), (512, 4), (2048, 16))
POOL_WINDOWS = (2, 4, 8, 16)
POOL_GROUP_DIM = 64
POOL_WIDTH = len(POOL_WINDOWS) * POOL_GROUP_DIM
DN_HEADS = 4
DN_HEAD_DIM = 128
DN_WIDTH = DN_HEADS * DN_HEAD_DIM
DN_CONV = 4
DN_CHUNK = 64
MIX_WIDTH = ATT_WIDTH + POOL_WIDTH + DN_WIDTH
IN_SPLITS = (ATT_WIDTH, ATT_WIDTH, ATT_WIDTH, POOL_WIDTH,
             DN_WIDTH, DN_WIDTH, DN_WIDTH, DN_WIDTH, DN_HEADS, DN_HEADS)
IN_WIDTH = sum(IN_SPLITS)
D_FF = 2816
ROPE_THETA = 10000.0
EPS = 1e-6

kernel_name = "hybrid_dilated_pool_deltanet_macaron"

def rms_norm(x, w):
    xf = x.astype(jnp.float32)
    y = xf * lax.rsqrt(jnp.mean(xf * xf, axis=-1, keepdims=True) + EPS)
    return (y * w).astype(x.dtype)

def swiglu(h, w_gate, w_up, w_down):
    return (jax.nn.silu(h @ w_gate) * (h @ w_up)) @ w_down

def rotary_tables(positions, dim):
    inv_freq = ROPE_THETA ** (-jnp.arange(0, dim, 2, dtype=jnp.float32) / dim)
    ang = positions.astype(jnp.float32)[..., None] * inv_freq
    return jnp.cos(ang)[:, :, None, :], jnp.sin(ang)[:, :, None, :]

def apply_rope(t, cos, sin):
    t1, t2 = jnp.split(t.astype(jnp.float32), 2, axis=-1)
    return jnp.concatenate([t1 * cos - t2 * sin, t2 * cos + t1 * sin], axis=-1).astype(t.dtype)

def dilated_window_attention(q, k, v, window, dilation):
    B, S, H, E = q.shape
    n = window // dilation
    span = n * dilation
    L = -(-S // span) * span
    M = L // dilation
    nb = M // n

    def to_blocks(t):
        t = jnp.pad(t, ((0, 0), (0, L - S), (0, 0), (0, 0)))
        return t.reshape(B, nb, n, dilation, H, E)

    def with_prev(t):
        prev = jnp.pad(t, ((0, 0), (1, 0), (0, 0), (0, 0), (0, 0), (0, 0)))[:, :-1]
        return jnp.concatenate([prev, t], axis=2)

    qb = to_blocks(q)
    kk = with_prev(to_blocks(k))
    vv = with_prev(to_blocks(v))
    s = jnp.einsum('bcqrhe,bckrhe->bcrhqk', qb, kk).astype(jnp.float32) / math.sqrt(E)
    qi = jnp.arange(n)[:, None]
    ki = jnp.arange(2 * n)[None, :]
    dist = n + qi - ki
    blk = jnp.arange(nb)[:, None, None]
    valid = (dist >= 0) & (dist <= n) & ((blk - 1) * n + ki >= 0)
    s = jnp.where(valid[None, :, None, None], s, -jnp.inf)
    m = jnp.max(s, axis=-1, keepdims=True)
    p = jnp.exp(s - m)
    den = jnp.sum(p, axis=-1, keepdims=True)
    o = jnp.einsum('bcrhqk,bckrhe->bcqrhe', (p / den).astype(vv.dtype), vv)
    lse = (m + jnp.log(den))[..., 0]
    o = o.reshape(B, L, H, E)[:, :S]
    lse = lse.transpose(0, 1, 4, 2, 3).reshape(B, L, H)[:, :S]
    return o, lse

def dilated_attention(q, k, v):
    outs, lses = [], []
    for window, dilation in DILATED_PATTERNS:
        o, lse = dilated_window_attention(q, k, v, window, dilation)
        outs.append(o)
        lses.append(lse)
    wts = jax.nn.softmax(jnp.stack(lses, axis=0), axis=0)
    y = sum(wts[i][..., None] * outs[i].astype(jnp.float32) for i in range(len(outs)))
    return y.astype(q.dtype)

def multiscale_pool(u, pool_w, pool_scale):
    B, S, _ = u.shape
    G = len(POOL_WINDOWS)
    ug = u.reshape(B, S, G, POOL_GROUP_DIM)
    cs = jnp.cumsum(ug.astype(jnp.float32), axis=1)
    t = jnp.arange(S)
    pooled = []
    for g, w in enumerate(POOL_WINDOWS):
        csg = cs[:, :, g]
        lower = jnp.pad(csg, ((0, 0), (w, 0), (0, 0)))[:, :S]
        count = jnp.minimum(t + 1, w).astype(jnp.float32)[None, :, None]
        pooled.append((csg - lower) / count)
    pooled = jnp.stack(pooled, axis=2) - ug.astype(jnp.float32)
    y = jnp.einsum('bsgc,gcd->bsgd', pooled.astype(u.dtype), pool_w)
    return y.reshape(B, S, POOL_WIDTH) * pool_scale

def causal_depthwise_conv(u, w):
    K = w.shape[0]
    up = jnp.pad(u, ((0, 0), (K - 1, 0), (0, 0)))
    return lax.conv_general_dilated(up, w[:, None, :], window_strides=(1,), padding='VALID',
                                    dimension_numbers=('NWC', 'WIO', 'NWC'),
                                    feature_group_count=u.shape[-1])

def l2_normalize(t):
    tf = t.astype(jnp.float32)
    return tf * lax.rsqrt(jnp.sum(tf * tf, axis=-1, keepdims=True) + EPS)

def chunk_gated_delta_rule(q, k, v, g, beta):
    B, S, H, Dk = q.shape
    Dv = v.shape[-1]
    C = DN_CHUNK
    N = S // C
    to_c = lambda t: t.astype(jnp.float32).reshape(B, N, C, H, -1).transpose(1, 0, 3, 2, 4)
    qc, kc, vc = to_c(q), to_c(k), to_c(v)
    beta = beta.astype(jnp.float32).reshape(B, N, C, H).transpose(1, 0, 3, 2)
    g = jnp.cumsum(g.astype(jnp.float32).reshape(B, N, C, H).transpose(1, 0, 3, 2), axis=-1)
    kb = kc * beta[..., None]
    vb = vc * beta[..., None]
    lower = jnp.tril(jnp.ones((C, C), dtype=bool))
    strict = jnp.tril(jnp.ones((C, C), dtype=bool), -1)
    diff = g[..., :, None] - g[..., None, :]
    decay = jnp.where(lower, jnp.exp(jnp.where(lower, diff, 0.0)), 0.0)
    A = jnp.where(strict, jnp.einsum('nbhid,nbhjd->nbhij', kb, kc) * decay, 0.0)
    eye = jnp.eye(C, dtype=jnp.float32)
    T = lax.linalg.triangular_solve(eye + A, jnp.broadcast_to(eye, A.shape),
                                    left_side=True, lower=True)
    u = T @ vb
    w = T @ (kb * jnp.exp(g)[..., None])
    intra = jnp.where(lower, jnp.einsum('nbhid,nbhjd->nbhij', qc, kc) * decay, 0.0)

    def step(state, xs):
        q_i, k_i, u_i, w_i, g_i, a_i = xs
        v_new = u_i - w_i @ state
        o = (q_i * jnp.exp(g_i)[..., None]) @ state + a_i @ v_new
        g_last = g_i[..., -1]
        k_dec = k_i * jnp.exp(g_last[..., None] - g_i)[..., None]
        state = state * jnp.exp(g_last)[..., None, None] + jnp.einsum('bhck,bhcv->bhkv', k_dec, v_new)
        return state, o

    state0 = jnp.zeros((B, H, Dk, Dv), dtype=jnp.float32)
    _, o = lax.scan(step, state0, (qc, kc, u, w, g, intra))
    return o.transpose(1, 0, 3, 2, 4).reshape(B, S, H, Dv)

def gated_deltanet(q, k, v, z, b, a, conv_w, a_log, dt_bias, norm_w):
    B, S, _ = q.shape
    qkv = jax.nn.silu(causal_depthwise_conv(jnp.concatenate([q, k, v], axis=-1), conv_w))
    q, k, v = jnp.split(qkv, 3, axis=-1)
    q = l2_normalize(q.reshape(B, S, DN_HEADS, DN_HEAD_DIM)) * (DN_HEAD_DIM ** -0.5)
    k = l2_normalize(k.reshape(B, S, DN_HEADS, DN_HEAD_DIM))
    v = v.reshape(B, S, DN_HEADS, DN_HEAD_DIM)
    beta = jax.nn.sigmoid(b.astype(jnp.float32))
    g = -jnp.exp(a_log.astype(jnp.float32)) * jax.nn.softplus(a.astype(jnp.float32) + dt_bias)
    o = chunk_gated_delta_rule(q, k, v, g, beta)
    o = rms_norm(o, norm_w) * jax.nn.silu(z.reshape(B, S, DN_HEADS, DN_HEAD_DIM).astype(jnp.float32))
    return o.reshape(B, S, DN_WIDTH).astype(z.dtype)

def setup_inputs(seed: int = 0) -> dict:
    key = jax.random.key(seed)
    ks = jax.random.split(key, 24)
    nrm = lambda kk, shape, fan_in: jax.random.normal(kk, shape, jnp.float32) * (fan_in ** -0.5)
    gain = lambda kk, shape: 1.0 + 0.05 * jax.random.normal(kk, shape, jnp.float32)
    L = DEPTH
    x = jax.random.normal(ks[0], (BATCH, SEQ, D_MODEL), jnp.float32)
    positions = jnp.broadcast_to(jnp.arange(SEQ, dtype=jnp.int32), (BATCH, SEQ))
    dt = jnp.exp(jax.random.uniform(ks[12], (L, DN_HEADS), jnp.float32,
                                    math.log(1e-3), math.log(1e-1)))
    dt_bias = dt + jnp.log(-jnp.expm1(-dt))
    a_log = jnp.log(jax.random.uniform(ks[11], (L, DN_HEADS), jnp.float32, 1.0, 16.0))
    return {
        "x": x,
        "positions": positions,
        "ffn1_norm": gain(ks[1], (L, D_MODEL)),
        "ffn1_w_gate": nrm(ks[2], (L, D_MODEL, D_FF), D_MODEL),
        "ffn1_w_up": nrm(ks[3], (L, D_MODEL, D_FF), D_MODEL),
        "ffn1_w_down": nrm(ks[4], (L, D_FF, D_MODEL), D_FF),
        "mix_norm": gain(ks[5], (L, D_MODEL)),
        "w_in": nrm(ks[6], (L, D_MODEL, IN_WIDTH), D_MODEL),
        "pool_w": nrm(ks[7], (L, len(POOL_WINDOWS), POOL_GROUP_DIM, POOL_GROUP_DIM), POOL_GROUP_DIM),
        "pool_scale": gain(ks[8], (L, POOL_WIDTH)),
        "dn_conv_w": nrm(ks[9], (L, DN_CONV, 3 * DN_WIDTH), DN_CONV),
        "dn_a_log": a_log,
        "dn_dt_bias": dt_bias,
        "dn_out_norm": gain(ks[13], (L, DN_HEAD_DIM)),
        "w_out": nrm(ks[14], (L, MIX_WIDTH, D_MODEL), MIX_WIDTH),
        "ffn2_norm": gain(ks[15], (L, D_MODEL)),
        "ffn2_w_gate": nrm(ks[16], (L, D_MODEL, D_FF), D_MODEL),
        "ffn2_w_up": nrm(ks[17], (L, D_MODEL, D_FF), D_MODEL),
        "ffn2_w_down": nrm(ks[18], (L, D_FF, D_MODEL), D_FF),
        "final_norm": gain(ks[19], (D_MODEL,)),
    }

def reference(x, positions, ffn1_norm, ffn1_w_gate, ffn1_w_up, ffn1_w_down, mix_norm, w_in,
              pool_w, pool_scale, dn_conv_w, dn_a_log, dn_dt_bias, dn_out_norm, w_out,
              ffn2_norm, ffn2_w_gate, ffn2_w_up, ffn2_w_down, final_norm):
    B, S, _ = x.shape
    cos, sin = rotary_tables(positions, ATT_HEAD_DIM)
    split_at = np.cumsum(IN_SPLITS)[:-1].tolist()
    for l in range(DEPTH):
        h = rms_norm(x, ffn1_norm[l])
        x = x + 0.5 * swiglu(h, ffn1_w_gate[l], ffn1_w_up[l], ffn1_w_down[l])
        h = rms_norm(x, mix_norm[l])
        proj = h @ w_in[l]
        aq, ak, av, pu, dq, dk, dv, dz, db, da = jnp.split(proj, split_at, axis=-1)
        aq = apply_rope(aq.reshape(B, S, ATT_HEADS, ATT_HEAD_DIM), cos, sin)
        ak = apply_rope(ak.reshape(B, S, ATT_HEADS, ATT_HEAD_DIM), cos, sin)
        av = av.reshape(B, S, ATT_HEADS, ATT_HEAD_DIM)
        ya = dilated_attention(aq, ak, av).reshape(B, S, ATT_WIDTH)
        yb = multiscale_pool(pu, pool_w[l], pool_scale[l])
        yc = gated_deltanet(dq, dk, dv, dz, db, da, dn_conv_w[l], dn_a_log[l],
                            dn_dt_bias[l], dn_out_norm[l])
        x = x + jnp.concatenate([ya, yb, yc], axis=-1) @ w_out[l]
        h = rms_norm(x, ffn2_norm[l])
        x = x + 0.5 * swiglu(h, ffn2_w_gate[l], ffn2_w_up[l], ffn2_w_down[l])
    return rms_norm(x, final_norm)


_drawn_inputs = setup_inputs


def setup_inputs(seed=0):
    import zlib

    import numpy as np

    out = dict(_drawn_inputs(seed))
    spreads = {}
    factors = {}
    for name, (base, spread) in spreads.items():
        noise = np.random.default_rng([zlib.crc32(name.encode()), seed]).standard_normal(out[name].shape)
        drawn = base * np.exp(spread * noise) if base else spread * noise
        out[name] = jnp.asarray(drawn.astype(out[name].dtype))
    for name, factor in factors.items():
        out[name] = (out[name] * factor).astype(out[name].dtype)
    return out
```

```python
from contextlib import ExitStack

import numpy as np

import concourse.bass as bass
from concourse import mybir

F32 = mybir.dt.float32
F32R = mybir.dt.float32r
I32 = mybir.dt.int32
ALU = mybir.AluOpType
ACT = mybir.ActivationFunctionType
AX = mybir.AxisListType

P = 128
D_MODEL = 1024
SEQ = 256
DEPTH = 2
D_FF = 2816
EPS = 1e-6
HALVES = SEQ // P
KT = D_MODEL // P
TILES = D_FF // P
NW = 512

ATT_HEADS, ATT_DIM = 4, 64
ATT_SCALE = ATT_DIM ** -0.5
PATTERNS = ((128, 1), (512, 4), (2048, 16))
POOL_WINDOWS = (2, 4, 8, 16)
POOL_DIM = 64
DN_HEADS = 4
DN_SCALE = 128 ** -0.5
TAPS = 4
UNITS = HALVES * DN_HEADS
ROPE_THETA = 10000.0

COL_AQ, COL_DQ, COL_DK, COL_DV, COL_DZ, IN_WIDTH = 0, 1024, 1536, 2048, 2560, 3080
GATES = 2 * DN_HEADS

SLOTS = 6
IN_PIECES = ([("qk", h, j) for h in range(DN_HEADS) for j in range(2)] + [("gates", 0, 0)]
             + [("v", h, 0) for h in range(DN_HEADS)] + [("z", h, 0) for h in range(DN_HEADS)])
N_IN_B = len(IN_PIECES)
ATT_PIECES = 2 * ATT_HEADS * ATT_DIM * 2 // P
ATT_GROUPS = [(0, 3), (3, 3), (6, 2)]
OUT_PIECES = KT
MIX_SLOTS = ([i % SLOTS for i in range(N_IN_B)] + [i % SLOTS for i in range(ATT_PIECES)]
             + [(4 + i) % SLOTS for i in range(OUT_PIECES)])
FIRST_ATT = N_IN_B
FIRST_OUT = N_IN_B + ATT_PIECES
MIX_PIECES = len(MIX_SLOTS)
FFN_PIECES = 3 * TILES
LAYER_PIECES = 2 * FFN_PIECES + MIX_PIECES
MIX_BASE = FFN_PIECES
FFN_BASE = (0, FFN_PIECES + MIX_PIECES)
SLOT_USES_MIX = [MIX_SLOTS.count(s) for s in range(SLOTS)]
SLOT_USES_FFN = TILES // 2
SLOT_USES = [2 * SLOT_USES_FFN + n for n in SLOT_USES_MIX]


def tap_row(i):
    return (i % 2) * DN_HEADS + i // 2 if i < 2 * DN_HEADS else i


def mix_occupant(i):
    for q in range(i - 1, -1, -1):
        if MIX_SLOTS[q] == MIX_SLOTS[i]:
            return q
    return -1


LEVELS = (2, 4, 8, 16, 32, 64)

C_IDENT = 0
C_FREQ = C_IDENT + P
C_FIRST = C_FREQ + ATT_DIM // 2
C_TRI = C_FIRST
C_NEG = C_TRI + P
C_PAIR = C_NEG + P
C_LEVEL = C_PAIR + P
C_ONES = C_LEVEL + P * len(LEVELS)
C_ATT = C_ONES + P
C_POOL = C_ATT + 3 * P
C_END = C_POOL + len(POOL_WINDOWS) * (SEQ + P)

R_CONV = 0
R_PSCALE = R_CONV + TAPS * 3 * DN_HEADS
R_ONORM = R_PSCALE + 2
R_END = R_ONORM + 1


def constants():
    c = np.zeros((P, C_END), np.float32)
    r, k = np.arange(P)[:, None], np.arange(P)[None, :]
    c[:, C_IDENT:C_IDENT + P] = r == k
    c[:, C_TRI:C_TRI + P] = r <= k
    c[:, C_NEG:C_NEG + P] = np.where(r <= k, 0.0, -1e30)
    c[:, C_PAIR:C_PAIR + P] = np.where(r == k, 1.0, np.where((r % 2 == 0) & (k == r + 1), -1.0, 0.0))
    for n, s in enumerate(LEVELS):
        below = ((r // s) % 2 == 1) & (k // s == r // s - 1)
        c[:, C_LEVEL + n * P:C_LEVEL + (n + 1) * P] = np.where(r == k, 1.0, np.where(below, -1.0, 0.0))
    c[:, C_ONES:C_ONES + P] = 1.0
    for n, away in enumerate((0, P, 0)):
        d = away + r - k
        count = np.zeros_like(d)
        for window, dilation in PATTERNS:
            count = count + ((d >= 0) & (d <= window) & (d % dilation == 0))
        c[:, C_ATT + n * P:C_ATT + (n + 1) * P] = np.where(count > 0, np.log(np.maximum(count, 1)), -1e30)
    for g, w in enumerate(POOL_WINDOWS):
        s, t = np.arange(SEQ)[:, None], np.arange(SEQ)[None, :]
        m = np.where((t >= s) & (t - s < w), 1.0 / np.minimum(t + 1, w), 0.0) - (s == t)
        at = C_POOL + g * (SEQ + P)
        c[:, at:at + SEQ] = m[:P]
        c[:, at + SEQ:at + SEQ + P] = m[P:, P:]
    half = ATT_DIM // 2
    c[:, C_FREQ:C_FREQ + half] = (np.float32(ROPE_THETA) ** (-np.arange(0, ATT_DIM, 2, dtype=np.float32)
                                                             / np.float32(ATT_DIM)))[None, :]
    return c


class Signal:

    def __init__(self, sem, per_layer, start=0):
        self.sem, self.per_layer, self.start = sem, per_layer, start

    def at(self, layer, n):
        return self.sem, layer * self.per_layer + n + self.start


def build(nc, x, positions, ffn1_norm, ffn1_w_gate, ffn1_w_up, ffn1_w_down, mix_norm, w_in, pool_w,
          pool_scale, dn_conv_w, dn_a_log, dn_dt_bias, dn_out_norm, w_out, ffn2_norm, ffn2_w_gate,
          ffn2_w_up, ffn2_w_down, final_norm, consts, out):
    ctx = ExitStack()
    with ctx:
        def sb(name, shape, dt=F32):
            return ctx.enter_context(nc.sbuf_tensor(name, shape, dt))

        def signal(name, per_layer=0, start=0):
            return Signal(ctx.enter_context(nc.semaphore(name)), per_layer, start)

        cst = sb("cst", [P, C_END])
        xr = sb("xr", [P, HALVES, D_MODEL])
        Xh = sb("Xh", [P, KT, SEQ], F32R)
        Xl = sb("Xl", [P, KT, SEQ], F32R)
        raw = sb("raw", [P, SLOTS, D_MODEL])
        Wh = sb("Wh", [P, SLOTS, D_MODEL], F32R)
        Wl = sb("Wl", [P, SLOTS, D_MODEL], F32R)
        aH = sb("aH", [P, 2, SEQ], F32R)
        aL = sb("aL", [P, 2, SEQ], F32R)
        gact = sb("gact", [P, 2, SEQ])
        hid = sb("hid", [P, 2, SEQ])
        norm_w = sb("norm_w", [P, D_MODEL])
        stat = sb("stat", [P, HALVES, 8])
        bias = sb("bias", [P, 2])
        prm_rows = sb("prm_rows", [R_END, DEPTH, P])
        prm_all = sb("prm_all", [P, DEPTH, R_END])
        prm = sb("prm", [P, R_END])
        dt_all = sb("dt_all", [P, DEPTH, DN_HEADS])
        al_all = sb("al_all", [P, DEPTH, DN_HEADS])
        pos_i = sb("pos_i", [P, HALVES], I32)
        pos_f = sb("pos_f", [P, HALVES])
        cosd = sb("cosd", [P, HALVES, ATT_DIM])
        sind = sb("sind", [P, HALVES, ATT_DIM])

        QK = sb("QK", [P, DN_HEADS, 2, SEQ])
        VT = sb("VT", [P, DN_HEADS, SEQ])
        SZ = sb("SZ", [P, DN_HEADS, SEQ])
        early = sb("early", [P, 10 * 256])
        sq = early[:, 0:1536].rearrange("p (b t) -> p b t", b=3)
        inv = early[:, 1536:2560].rearrange("p (b t) -> p b t", b=2)
        V = early[:, 0:1024].rearrange("p (u d) -> p u d", u=UNITS)
        Kn = early[:, 1024:1536].rearrange("p (h d) -> p h d", h=DN_HEADS)
        Vd = early[:, 1536:2048].rearrange("p (h d) -> p h d", h=DN_HEADS)
        St = early[:, 2048:2560].rearrange("p (h d) -> p h d", h=DN_HEADS)
        ang = early[:, 0:768].rearrange("p (n t) -> p n t", n=6)
        big = sb("big", [P, HALVES, D_MODEL])
        dec = sb("dec", [P, UNITS, P])
        grow = sb("grow", [P, UNITS, P])
        LT = sb("LT", [P, UNITS, P])
        aT = sb("aT", [P, UNITS, P])
        Dm = sb("Dm", [P, UNITS, P])
        DT = sb("DT", [P, UNITS, P])
        PM = sb("PM", [P, UNITS, P])
        qkr = sb("qkr", [P, HALVES, 512])
        rtmp = VT[:, :, :].rearrange("p (c a) t -> p c (a t)", c=HALVES)
        qT = sb("qT", [P, 2, SEQ])
        kT = sb("kT", [P, 2, SEQ])
        pr = sb("pr", [P, 2, 3 * P])
        prT = sb("prT", [P, 2, 3 * P])
        pooled = sb("pooled", [P, 2, SEQ])
        pw = sb("pw", [P, DEPTH, 2, POOL_DIM])
        pwl = sb("pwl", [P, 2, POOL_DIM])
        mx = sb("mx", [P, ATT_HEADS, 2])
        sm = sb("sm", [P, ATT_HEADS, 2])
        rc = sb("rc", [P, ATT_HEADS, 2])
        ost = sb("ost", [P, HALVES, 8, DN_HEADS])
        ga = sb("ga", [P, 20, 16])
        O, Vn = grow, LT
        Dsq = qkr[:, 0, :]
        R1, QS = Dm[:, 0:4, :], Dm[:, 4:8, :]
        Yf = PM

        bank = [ctx.enter_context(nc.psum_tensor(f"bank{i}", [P, NW], F32)) for i in range(8)]
        acc = [[bank[0], bank[1]], [bank[2], bank[3]]]
        gbank, ubank = [bank[4], bank[6]], [bank[5], bank[7]]
        tbank = [bank[4], bank[5], bank[6], bank[7]]

        ident = cst[:, C_IDENT:C_IDENT + P]
        tri = cst[:, C_TRI:C_TRI + P]
        neg = cst[:, C_NEG:C_NEG + P]
        ones = cst[:, C_ONES:C_ONES + P]
        att_mask = cst[:, C_ATT:C_ATT + 3 * P]

        consts_in = signal("consts_in")
        x_in = [signal(f"x_in{c}") for c in range(HALVES)]
        masks_in = signal("masks_in")
        rows_in = signal("rows_in")
        small_in = signal("small_in")
        zeroed = signal("zeroed")
        prm_turned = signal("prm_turned")
        prologue = signal("prologue")
        pro_step = signal("pro_step")
        trig = signal("trig")
        out_ready = signal("out_ready")
        out_written = signal("out_written")
        landed = [signal(f"landed{s}", 16 * SLOT_USES[s]) for s in range(SLOTS)]
        hi_cast = signal("hi_cast", LAYER_PIECES)
        lo_cast = signal("lo_cast", LAYER_PIECES, SLOTS)
        out_used = signal("out_used", OUT_PIECES)
        norm_w_in = signal("norm_w_in", 16 * 3)
        x_new = signal("x_new", 12, 0)
        ss_done = signal("ss_done", 6)
        ln_done = signal("ln_done", 6)
        rs_done = signal("rs_done", 6)
        newton = signal("newton", 24)
        rows_normed = signal("rows_normed", 6, 2)
        turned = signal("turned", 12)
        xh_done = signal("xh_done", 12)
        xl_done = signal("xl_done", 12)
        gates_done = signal("gates_done", 2 * TILES, 2)
        ups_done = signal("ups_done", 2 * TILES, 2)
        downs_done = signal("downs_done", 2 * TILES, 2)
        silu_done = signal("silu_done", 2 * TILES, 2)
        mul_done = signal("mul_done", 2 * TILES, 2)
        ah_done = signal("ah_done", 2 * TILES, 2)
        al_done = signal("al_done", 2 * TILES, 2)
        acc_half = signal("acc_half", 3)
        prm_set = signal("prm_set", 1)
        proj = signal("proj", 16)
        conv1 = signal("conv1", 12)
        conv_mid = signal("conv_mid", 24)
        convd = signal("convd", 12)
        conv_act = signal("conv_act", 12)
        z_act = signal("z_act", 4)
        squared = signal("squared", 4)
        sumsq = signal("sumsq", 4)
        ln2 = signal("ln2", 4)
        inv_done = signal("inv_done", 4)
        normed = signal("normed", 4)
        gates_in = signal("gates_in", 1)
        gstep = signal("gstep", 16)
        gexp = signal("gexp", 1)
        gln = signal("gln", 1)
        tri_g = signal("tri_g", 1)
        cum_col = signal("cum_col", 1)
        cum_row = signal("cum_row", 2)
        cum_read = signal("cum_read", 1)
        eg_done = signal("eg_done", 1)
        neg_eg = signal("neg_eg", 1)
        diff_done = signal("diff_done", 2)
        decayed = signal("decayed", 2)
        gram = signal("gram", 4)
        lt_raw = signal("lt_raw", 4)
        lt_seen = signal("lt_seen", 2)
        at_done = signal("at_done", 4)
        lt_done = signal("lt_done", 2)
        dt0_done = signal("dt0_done", 2)
        d0_turned = signal("d0_turned", 2)
        d_done = signal("d_done", 2 * len(LEVELS))
        p_done = signal("p_done", 2 * len(LEVELS))
        pm_done = signal("pm_done", 2 * len(LEVELS))
        dd_done = signal("dd_done", 2 * len(LEVELS))
        dt_done = signal("dt_done", 2 * len(LEVELS))
        v_turned = signal("v_turned", 2)
        v_copied = signal("v_copied", 2)
        k_turned = signal("k_turned", 1)
        k_copied = signal("k_copied", 1)
        vn_ps = signal("vn_ps", 2)
        vn_done = signal("vn_done", 2)
        vd_done = signal("vd_done", 1)
        st_ps = signal("st_ps", 1)
        st_done = signal("st_done", 1)
        ks_ps = signal("ks_ps", 1)
        qs_ps = signal("qs_ps", 1)
        r1_done = signal("r1_done", 1)
        qs_done = signal("qs_done", 1)
        o_ps = signal("o_ps", 2)
        o_done = signal("o_done", 2)
        o_sq = signal("o_sq", 2)
        o_ss = signal("o_ss", 2)
        o_var = signal("o_var", 2)
        o_ln = signal("o_ln", 2)
        o_rs = signal("o_rs", 2)
        o_newton = signal("o_newton", 6)
        o_newton2 = signal("o_newton2", 2)
        o_normed = signal("o_normed", 2)
        o_turned = signal("o_turned", 2)
        y_gated = signal("y_gated", 2)
        y_hi = signal("y_hi", 2)
        y_lo = signal("y_lo", 2)
        att_in = signal("att_in", 6)
        att_read = signal("att_read", 6)
        rope_cos = signal("rope_cos", 2)
        rope_sin = signal("rope_sin", 2)
        roped = signal("roped", 4)
        qk_turned = signal("qk_turned", 2)
        qk_copied = signal("qk_copied", 2)
        scored = signal("scored", 4)
        masked = signal("masked", 4)
        maxed = signal("maxed", 4)
        exped = signal("exped", 8)
        recip = signal("recip", 4)
        weighted = signal("weighted", 4)
        pr_turned = signal("pr_turned", 4)
        pr_copied = signal("pr_copied", 4)
        att_out = signal("att_out", 2)
        att_hi = signal("att_hi", 2)
        att_lo = signal("att_lo", 2)
        pool_ps = signal("pool_ps", 2)
        pool_copied = signal("pool_copied", 2)
        pool_out = signal("pool_out", 2)
        pool_hi = signal("pool_hi", 2)
        pool_lo = signal("pool_lo", 2)

        FFN = ((ffn1_w_gate, ffn1_w_up, ffn1_w_down), (ffn2_w_gate, ffn2_w_up, ffn2_w_down))

        def cols(ap, layer, first, width=P):
            return ap[layer, :, bass.ds(first, width)].rearrange("(k p) c -> p k c", p=P)

        def piece(t, s):
            return t[:, s, :].rearrange("p (k c) -> p k c", k=KT)

        block = ctx.enter_context(nc.Block())

        @block.sync
        def _(sp):
            for c in range(HALVES):
                sp.dma_start(xr[:, c, :], x[0, c * P:(c + 1) * P, :]).then_inc(x_in[c].sem, 16)
            sp.dma_start(cst[:, 0:C_FIRST], consts[:, 0:C_FIRST]).then_inc(consts_in.sem, 16)

            def load_norm(layer, n, src):
                sp.wait_ge(*rows_normed.at(layer, 2 * n))
                sp.dma_start(norm_w[:, :], src.partition_broadcast(P)).then_inc(norm_w_in.sem, 16)

            def load(layer, index, s, src, dst):
                sp.wait_ge(*lo_cast.at(layer, index - SLOTS + 1))
                sp.dma_start(dst, src).then_inc(landed[s].sem, 16)

            def load_tile(layer, f, t, par):
                gate, up, down = FFN[f]
                base = FFN_BASE[f]
                s = 3 * par
                load(layer, t * 3 + base, s, cols(gate, layer, t * P), piece(raw, s))
                load(layer, t * 3 + (base + 1), s + 1, cols(up, layer, t * P), piece(raw, s + 1))
                load(layer, t * 3 + (base + 2), s + 2, down[layer, bass.ds(t * P, P), :], raw[:, s + 2, :])

            def load_ffn(layer, f):
                if f == 1:
                    gate, up, down = FFN[f]
                    for t in range(2):
                        srcs = (cols(gate, layer, t * P), cols(up, layer, t * P), down[layer, t * P:(t + 1) * P, :])
                        for j in range(3):
                            s = 3 * t + j
                            last = max(i for i in range(MIX_PIECES) if MIX_SLOTS[i] == s)
                            sp.wait_ge(*lo_cast.at(layer, MIX_BASE + last + 1))
                            sp.dma_start(raw[:, s, :] if j == 2 else piece(raw, s), srcs[j]).then_inc(landed[s].sem, 16)
                    with sp.Fori(1, TILES // 2) as g:
                        load_tile(layer, f, g * 2, 0)
                        load_tile(layer, f, g * 2 + 1, 1)
                else:
                    with sp.Fori(0, TILES // 2) as g:
                        load_tile(layer, f, g * 2, 0)
                        load_tile(layer, f, g * 2 + 1, 1)

            with sp.Fori(0, DEPTH) as layer:
                load_norm(layer, 0, ffn1_norm[bass.ds(layer, 1), :].squeeze(0))
                load_ffn(layer, 0)
                load_norm(layer, 1, mix_norm[bass.ds(layer, 1), :].squeeze(0))
                order = list(range(MIX_PIECES))
                order[FIRST_ATT:FIRST_ATT + 2] = [FIRST_ATT + 1, FIRST_ATT]
                for i in order:
                    s, q = MIX_SLOTS[i], mix_occupant(i)
                    if i != FIRST_ATT:
                        sp.wait_ge(*lo_cast.at(layer, MIX_BASE + q + 1 if q >= 0
                                               else FFN_BASE[0] + FFN_PIECES - SLOTS + s + 1))
                    if i < FIRST_ATT:
                        kind, h, j = IN_PIECES[i]
                        first = {"qk": (COL_DQ, COL_DK)[j] + h * P, "gates": IN_WIDTH - P,
                                 "v": COL_DV + h * P, "z": COL_DZ + h * P}[kind]
                        src, dst = cols(w_in, layer, first), piece(raw, s)
                    elif i < FIRST_OUT:
                        src, dst = cols(w_in, layer, COL_AQ + (i - FIRST_ATT) * P), piece(raw, s)
                    else:
                        k = i - FIRST_OUT
                        src, dst = w_out[layer, k * P:(k + 1) * P, :], raw[:, s, :]
                    sp.dma_start(dst, src).then_inc(landed[s].sem, 16)
                load_norm(layer, 2, ffn2_norm[bass.ds(layer, 1), :].squeeze(0))
                load_ffn(layer, 1)

            load_norm(DEPTH, 0, final_norm)
            sp.wait_ge(out_ready.sem, 1)
            sp.dma_start(out[0, 0:P, :], big[:, 0, :]).then_inc(out_written.sem, 16)
            sp.wait_ge(out_ready.sem, 2)
            sp.dma_start(out[0, P:SEQ, :], big[:, 1, :]).then_inc(out_written.sem, 16)
            sp.wait_ge(out_written.sem, 32)

        @block.gpsimd
        def _(pool):
            one = pool.to_reg(1.0)
            with pool.Fori(0, DEPTH) as layer:
                for c in range(HALVES):
                    pool.wait_ge(*lt_raw.at(layer, 2 * c + 2))
                    pool.sem_inc(lt_seen.sem, 1)
                    u = LT[:, 4 * c:4 * c + 4, :]
                    nc.gpsimd.affine_select(out=u, in_=u, compare_op=ALU.not_equal, fill=one, base=0,
                                            pattern=[[0, 4], [-1, P]],
                                            channel_multiplier=1).then_inc(lt_done.sem, 1)
                for c in range(HALVES):
                    for g in range(2):
                        pool.wait_ge(*att_read.at(layer, 2 * g + c + 1))
                    a8 = big[:, c, 0:512].rearrange("p (h e) -> p h e", e=ATT_DIM)
                    o8 = qkr[:, c, :].rearrange("p (h e) -> p h e", e=ATT_DIM)
                    t8 = rtmp[:, c, :].rearrange("p (h e) -> p h e", e=ATT_DIM)
                    cb = cosd[:, c, :].unsqueeze(1).broadcast_to([P, 8, ATT_DIM])
                    sbd = sind[:, c, :].unsqueeze(1).broadcast_to([P, 8, ATT_DIM])
                    nc.gpsimd.tensor_tensor(o8, a8, cb, ALU.mult).then_inc(rope_cos.sem, 1)
                    nc.gpsimd.tensor_tensor(t8, a8, sbd, ALU.mult).then_inc(rope_sin.sem, 1)
                    pool.wait_ge(*rope_cos.at(layer, c + 1))
                    pool.wait_ge(*rope_sin.at(layer, c + 1))
                    h = ATT_DIM // 2
                    nc.gpsimd.tensor_tensor(o8[:, :, 0:h], o8[:, :, 0:h], t8[:, :, h:],
                                            ALU.subtract).then_inc(roped.sem, 1)
                    nc.gpsimd.tensor_tensor(o8[:, :, h:], o8[:, :, h:], t8[:, :, 0:h],
                                            ALU.add).then_inc(roped.sem, 1)

        @block.tensor
        def _(pe):
            for s, n in ((gates_done, 2), (ups_done, 2), (downs_done, 2)):
                pe.sem_inc(s.sem, n)
            pe.wait_ge(consts_in.sem, 16)
            pe.wait_ge(rows_in.sem, 16 * 3)
            for l in range(DEPTH):
                nc.tensor.transpose(bank[0][:, l * P:l * P + R_END], prm_rows[:, l, :],
                                    cst[0:R_END, C_IDENT:C_IDENT + R_END]).then_inc(prm_turned.sem, 1)

            def three(outp, lh, ll, rh, rl, start, stop):
                nc.tensor.matmul(outp, lh, rh, start=start, stop=False)
                nc.tensor.matmul(outp, lh, rl, start=False, stop=False)
                return nc.tensor.matmul(outp, ll, rh, start=False, stop=stop)

            def turn_rows(layer, n):
                for c in range(HALVES):
                    pe.wait_ge(*rows_normed.at(layer, 2 * n + c + 1))
                    for b in range(2):
                        for k in range(4):
                            m = nc.tensor.transpose(tbank[2 * c + b][:, k * P:(k + 1) * P],
                                                    big[:, c, (4 * b + k) * P:(4 * b + k + 1) * P], ident)
                        m.then_inc(turned.sem, 1)

            def column_piece(outp, s):
                for k in range(KT):
                    m = three(outp, piece(Wh, s)[:, k, :], piece(Wl, s)[:, k, :], Xh[:, k, :], Xl[:, k, :],
                              k == 0, k == KT - 1)
                return m

            def gate_up(layer, f, t, par):
                T = t + f * TILES
                pe.wait_ge(*lo_cast.at(layer, t * 3 + (FFN_BASE[f] + 1)))
                pe.wait_ge(*silu_done.at(layer, T - 1))
                column_piece(gbank[par][:, 0:SEQ], 3 * par).then_inc(gates_done.sem, 1)
                pe.wait_ge(*lo_cast.at(layer, t * 3 + (FFN_BASE[f] + 2)))
                pe.wait_ge(*mul_done.at(layer, T - 1))
                column_piece(ubank[par][:, 0:SEQ], 3 * par + 1).then_inc(ups_done.sem, 1)

            def down(layer, f, t, par, first=False, last=False):
                T = t + f * TILES
                pe.wait_ge(*lo_cast.at(layer, t * 3 + (FFN_BASE[f] + 3)))
                pe.wait_ge(*al_done.at(layer, T + 1))
                s = 3 * par + 2
                for c in range(HALVES):
                    for n in range(2):
                        m = three(acc[c][n][:, :], aH[:, par, c * P:(c + 1) * P], aL[:, par, c * P:(c + 1) * P],
                                  Wh[:, s, n * NW:(n + 1) * NW], Wl[:, s, n * NW:(n + 1) * NW], first, last)
                    if last and c == 0:
                        m.then_inc(acc_half.sem, 1)
                m.then_inc(downs_done.sem, 1)

            def ffn(layer, f):
                pe.wait_ge(*xl_done.at(layer, 8 * f + 4))
                gate_up(layer, f, 0, 0)
                gate_up(layer, f, 1, 1)
                down(layer, f, 0, 0, first=True)
                with pe.Fori(0, TILES // 2 - 1) as g:
                    gate_up(layer, f, g * 2 + 2, 0)
                    down(layer, f, g * 2 + 1, 1)
                    gate_up(layer, f, g * 2 + 3, 1)
                    down(layer, f, g * 2 + 2, 0)
                down(layer, f, TILES - 1, 1, last=True)

            def mixer(layer):
                def split(i):
                    pe.wait_ge(*lo_cast.at(layer, MIX_BASE + i + 1))

                pe.wait_ge(*xl_done.at(layer, 8))
                for i in range(8):
                    split(i)
                    column_piece(bank[i][:, 0:SEQ], MIX_SLOTS[i]).then_inc(proj.sem, 1)
                split(8)
                pe.wait_ge(*convd.at(layer, 1))
                for c in range(HALVES):
                    for k in range(KT):
                        w = slice(P - GATES, P)
                        m = three(bank[0][:, c * GATES:(c + 1) * GATES], Xh[:, k, c * P:(c + 1) * P],
                                  Xl[:, k, c * P:(c + 1) * P], piece(Wh, MIX_SLOTS[8])[:, k, w],
                                  piece(Wl, MIX_SLOTS[8])[:, k, w], k == 0, k == KT - 1)
                m.then_inc(gates_in.sem, 1)
                for h in range(2):
                    split(9 + h)
                    pe.wait_ge(*convd.at(layer, 2 + h))
                    column_piece(bank[1 + h][:, 0:SEQ], MIX_SLOTS[9 + h]).then_inc(proj.sem, 1)
                for h in range(DN_HEADS):
                    pe.wait_ge(*squared.at(layer, h + 1))
                    pe.wait_ge(*convd.at(layer, 4 + h))
                    nc.tensor.matmul(bank[3 + h][:, :], ones, sq[:, h % 3, :], start=True,
                                     stop=True).then_inc(sumsq.sem, 1)
                for h in (2, 3):
                    split(9 + h)
                    if h == 2:
                        pe.wait_ge(*convd.at(layer, 8))
                    else:
                        pe.wait_ge(*gstep.at(layer, 1))
                    column_piece(bank[(5 + h) % 8][:, 0:SEQ], MIX_SLOTS[9 + h]).then_inc(proj.sem, 1)
                pe.wait_ge(*gstep.at(layer, 16))
                pe.wait_ge(*convd.at(layer, 9))
                nc.tensor.matmul(bank[1][:, 0:UNITS], tri, ga[:, 9, 0:UNITS], start=True,
                                 stop=True).then_inc(cum_col.sem, 1)
                pe.wait_ge(*tri_g.at(layer, 1))
                pe.wait_ge(*convd.at(layer, 10))
                pe.wait_ge(*ln2.at(layer, 1))
                for c in range(HALVES):
                    nc.tensor.matmul(bank[2 + c][:, :], ones, grow[:, 4 * c:4 * c + 4, :], start=True,
                                     stop=True).then_inc(cum_row.sem, 1)
                for h in range(2):
                    split(13 + h)
                    pe.wait_ge(*ln2.at(layer, 2 + h))
                    column_piece(bank[4 + h][:, 0:SEQ], MIX_SLOTS[13 + h]).then_inc(proj.sem, 1)
                for n in range(4):
                    b = bank[(6, 7, 0, 1)[n]]
                    if n == 0:
                        pe.wait_ge(*normed.at(layer, 4))
                        pe.wait_ge(*ln2.at(layer, 4))
                    if n == 1:
                        pe.wait_ge(*convd.at(layer, 11))
                    if n == 2:
                        pe.wait_ge(*convd.at(layer, 12))
                    if n == 3:
                        pe.wait_ge(*cum_read.at(layer, 1))
                    for j in range(2):
                        c, h = divmod(2 * n + j, DN_HEADS)
                        t = slice(c * P, (c + 1) * P)
                        m = nc.tensor.matmul(b[:, j * SEQ:(j + 1) * SEQ].rearrange("p (a t) -> p a t", a=2),
                                             QK[:, h, 1, t], QK[:, h, :, t], start=True, stop=True)
                    m.then_inc(gram.sem, 1)
                for h in (2, 3):
                    split(13 + h)
                    pe.wait_ge(*diff_done.at(layer, h - 1))
                    column_piece(bank[h][:, 0:SEQ], MIX_SLOTS[13 + h]).then_inc(proj.sem, 1)
                for c in range(HALVES):
                    pe.wait_ge(*conv_act.at(layer, 12))
                    pe.wait_ge(*at_done.at(layer, c + 1))
                    for h in range(DN_HEADS):
                        m = nc.tensor.transpose(bank[6 + c][:, h * P:(h + 1) * P], VT[:, h, c * P:(c + 1) * P], ident)
                    m.then_inc(v_turned.sem, 1)
                pe.wait_ge(*at_done.at(layer, 3))
                for h in range(DN_HEADS):
                    m = nc.tensor.transpose(bank[0][:, h * P:(h + 1) * P], QK[:, h, 1, 0:P], ident)
                m.then_inc(k_turned.sem, 1)
                for c in range(HALVES):
                    pe.wait_ge(*dt0_done.at(layer, c + 1))
                    pe.wait_ge(*z_act.at(layer, c + 1))
                    for h in range(DN_HEADS):
                        m = nc.tensor.transpose(bank[4 + c][:, h * P:(h + 1) * P], DT[:, 4 * c + h, :], ident)
                    m.then_inc(d0_turned.sem, 1)
                abank = [bank[2], bank[3], bank[1], bank[0], bank[2], bank[3]]

                def att_group(g):
                    first, n = ATT_GROUPS[g]
                    split(FIRST_ATT + first + n - 1)
                    s0 = MIX_SLOTS[FIRST_ATT + first]
                    for c in range(HALVES):
                        j = 2 * g + c
                        if j < 2:
                            pe.wait_ge(*z_act.at(layer, 3 + j))
                        elif j == 2:
                            pe.wait_ge(*at_done.at(layer, 4))
                        elif j == 3:
                            pe.wait_ge(*k_copied.at(layer, 1))
                        else:
                            pe.wait_ge(*att_read.at(layer, j - 3))
                        b = abank[j][:, 0:n * P].rearrange("p (s c) -> p s c", s=n)
                        for k in range(KT):
                            rh = Wh[:, s0:s0 + n, k * P:(k + 1) * P]
                            rl = Wl[:, s0:s0 + n, k * P:(k + 1) * P]
                            m = three(b, Xh[:, k, c * P:(c + 1) * P], Xl[:, k, c * P:(c + 1) * P], rh, rl,
                                      k == 0, k == KT - 1)
                        m.then_inc(att_in.sem, 1)

                def level_p(n, c):
                    pe.wait_ge(*d_done.at(layer, 2 * n + c + 1))
                    if n == 0:
                        pe.wait_ge(*lt_done.at(layer, c + 1))
                    for h in range(DN_HEADS):
                        u = 4 * c + h
                        m = nc.tensor.matmul(bank[4 + c][:, h * P:(h + 1) * P], LT[:, u, :], Dm[:, u, :],
                                             start=True, stop=True)
                    m.then_inc(p_done.sem, 1)

                def level_d(n, c):
                    s = LEVELS[n]
                    pe.wait_ge(*pm_done.at(layer, 2 * n + c + 1))
                    if n == 0:
                        pe.wait_ge(*v_copied.at(layer, c + 1))
                    else:
                        pe.wait_ge(*dt_done.at(layer, 2 * n + c - 1))
                    b = bank[6 + c]
                    for h in range(DN_HEADS):
                        u = 4 * c + h
                        pm = PM[:, u, :].rearrange("p (n a s) -> p n a s", a=2, s=s)
                        dt = DT[:, u, :].rearrange("p (n a s) -> p n a s", a=2, s=s)
                        if n < len(LEVELS) - 1:
                            nc.tensor.matmul(b[:, h * 64:(h + 1) * 64].rearrange("p (n s) -> p n s", s=s),
                                             DT[:, u, :], pm[:, :, 0, :], start=True, stop=True)
                        m = nc.tensor.matmul(b[:, 256 + h * 64:256 + (h + 1) * 64]
                                             .rearrange("p (n s) -> p n s", s=s),
                                             PM[:, u, :], dt[:, :, 1, :], start=True, stop=True)
                    m.then_inc(dd_done.sem, 1)

                for n in range(len(LEVELS)):
                    for c in range(HALVES):
                        level_p(n, c)
                    for c in range(HALVES):
                        level_d(n, c)
                    if n in (0, 2, 4):
                        att_group(n // 2)

                pe.wait_ge(*dt_done.at(layer, 2 * len(LEVELS) - 1))
                pe.wait_ge(*pm_done.at(layer, 2 * len(LEVELS)))
                for h in range(DN_HEADS):
                    m = nc.tensor.matmul(bank[4][:, h * P:(h + 1) * P], DT[:, h, :], V[:, h, :], start=True, stop=True)
                m.then_inc(vn_ps.sem, 1)
                pe.wait_ge(*roped.at(layer, 4))
                for j in range(2):
                    if j == 1:
                        pe.wait_ge(*dt_done.at(layer, 2 * len(LEVELS)))
                    for c in range(HALVES):
                        for pair in range(2):
                            m = nc.tensor.transpose(bank[5 + j][:, pair * SEQ + c * P:pair * SEQ + (c + 1) * P],
                                                    qkr[:, c, j * 256 + pair * P:j * 256 + (pair + 1) * P], ident)
                    m.then_inc(qk_turned.sem, 1)
                pe.wait_ge(*vd_done.at(layer, 1))
                pe.wait_ge(*k_copied.at(layer, 1))
                for h in range(DN_HEADS):
                    m = nc.tensor.matmul(bank[7][:, h * P:(h + 1) * P], Kn[:, h, :], Vd[:, h, :], start=True, stop=True)
                m.then_inc(st_ps.sem, 1)
                pe.wait_ge(*vn_done.at(layer, 1))
                for h in range(DN_HEADS):
                    m = nc.tensor.matmul(bank[4][:, h * P:(h + 1) * P], aT[:, h, :], Vn[:, h, :], start=True, stop=True)
                m.then_inc(o_ps.sem, 1)
                pe.wait_ge(*st_done.at(layer, 1))
                pe.wait_ge(*qk_copied.at(layer, 2))
                for h in range(DN_HEADS):
                    m = nc.tensor.matmul(bank[5][:, h * P:(h + 1) * P], QK[:, h, 1, P:SEQ], St[:, h, :], start=True, stop=True)
                m.then_inc(ks_ps.sem, 1)
                for h in range(DN_HEADS):
                    m = nc.tensor.matmul(bank[6][:, h * P:(h + 1) * P], QK[:, h, 0, P:SEQ], St[:, h, :], start=True, stop=True)
                m.then_inc(qs_ps.sem, 1)

                def scores(h):
                    j, r = h // 2, (h % 2) * ATT_DIM
                    b = bank[h % 2]
                    if h >= 2:
                        pe.wait_ge(*masked.at(layer, h - 1))
                    else:
                        pe.wait_ge(*att_read.at(layer, 4 - h))
                    nc.tensor.matmul(b[:, 0:P], qT[r:r + ATT_DIM, j, 0:P], kT[r:r + ATT_DIM, j, 0:P],
                                     start=True, stop=True)
                    nc.tensor.matmul(b[:, P:3 * P], qT[r:r + ATT_DIM, j, P:SEQ], kT[r:r + ATT_DIM, j, :],
                                     start=True, stop=True).then_inc(scored.sem, 1)

                scores(0)
                scores(1)
                for j in range(2):
                    pe.wait_ge(*att_read.at(layer, 6))
                    for a in range(2):
                        g = 2 * j + a
                        at = C_POOL + g * (SEQ + P)
                        u = slice(768 + g * POOL_DIM, 768 + (g + 1) * POOL_DIM)
                        ob = bank[2 + j][a * POOL_DIM:(a + 1) * POOL_DIM, :]
                        nc.tensor.matmul(ob[:, 0:SEQ], big[:, 0, u], cst[:, at:at + SEQ], start=True, stop=False,
                                         skip_group_check=True)
                        m = nc.tensor.matmul(ob[:, P:SEQ], big[:, 1, u], cst[:, at + SEQ:at + SEQ + P],
                                             start=False, stop=True, skip_group_check=True)
                    m.then_inc(pool_ps.sem, 1)
                pe.wait_ge(*r1_done.at(layer, 1))
                for h in range(DN_HEADS):
                    m = nc.tensor.matmul(bank[7][:, h * P:(h + 1) * P], DT[:, 4 + h, :], R1[:, h, :], start=True, stop=True)
                m.then_inc(vn_ps.sem, 1)
                scores(2)
                scores(3)
                pe.wait_ge(*pool_copied.at(layer, 2))
                pe.wait_ge(*vn_done.at(layer, 2))
                pe.wait_ge(*qs_done.at(layer, 1))
                for h in range(DN_HEADS):
                    m = nc.tensor.matmul(bank[6][:, h * P:(h + 1) * P], aT[:, 4 + h, :], Vn[:, 4 + h, :], start=True, stop=True)
                m.then_inc(o_ps.sem, 1)

                for j in range(2):
                    for a in range(2):
                        r = slice(a * POOL_DIM, (a + 1) * POOL_DIM)
                        m = nc.tensor.matmul(bank[2 + j][r, 0:SEQ], pwl[r, j, :], pooled[r, j, :],
                                             start=True, stop=True)
                    m.then_inc(pool_out.sem, 1)
                def att_values(h):
                    j, r = h // 2, (h % 2) * ATT_DIM
                    pe.wait_ge(*weighted.at(layer, h + 1))
                    if h == 0:
                        pe.wait_ge(*vn_done.at(layer, 2))
                    else:
                        pe.wait_ge(*pr_copied.at(layer, h))
                    for n in range(3):
                        m = nc.tensor.transpose(bank[7][:, n * P:(n + 1) * P], pr[:, h % 2, n * P:(n + 1) * P], ident)
                    m.then_inc(pr_turned.sem, 1)
                    pe.wait_ge(*pr_copied.at(layer, h + 1))
                    if h == 0:
                        pe.wait_ge(*o_done.at(layer, 1))
                    if h == 2:
                        pe.wait_ge(*r1_done.at(layer, 1))
                    v = slice(512 + h * ATT_DIM, 512 + (h + 1) * ATT_DIM)
                    ob = bank[4 + j][r:r + ATT_DIM, :]
                    nc.tensor.matmul(ob[:, 0:P], big[:, 0, v], prT[:, h % 2, 0:P], start=True, stop=True)
                    nc.tensor.matmul(ob[:, P:SEQ], big[:, 0, v], prT[:, h % 2, P:2 * P], start=True, stop=False)
                    m = nc.tensor.matmul(ob[:, P:SEQ], big[:, 1, v], prT[:, h % 2, 2 * P:3 * P], start=False, stop=True)
                    if h % 2:
                        m.then_inc(att_out.sem, 1)

                for h in range(ATT_HEADS):
                    att_values(h)

                for c in range(HALVES):
                    pe.wait_ge(*o_normed.at(layer, c + 1))
                    if c == 0:
                        pe.wait_ge(*o_done.at(layer, 2))
                    else:
                        pe.wait_ge(*pr_copied.at(layer, 4))
                    for h in range(DN_HEADS):
                        m = nc.tensor.transpose(bank[6 + c][:, h * P:(h + 1) * P], O[:, 4 * c + h, :], ident)
                    m.then_inc(o_turned.sem, 1)

                for k in range(KT):
                    i = FIRST_OUT + k
                    split(i)
                    if k < 2:
                        pe.wait_ge(*att_lo.at(layer, k + 1))
                    elif k < 4:
                        pe.wait_ge(*pool_lo.at(layer, k - 1))
                    if k == 0:
                        pe.wait_ge(*masked.at(layer, 4))
                        pe.wait_ge(*pool_lo.at(layer, 2))
                    if k == 4:
                        pe.wait_ge(*y_lo.at(layer, 2))
                    s = MIX_SLOTS[i]
                    for c in range(HALVES):
                        for n in range(2):
                            m = three(acc[c][n][:, :], Xh[:, k, c * P:(c + 1) * P], Xl[:, k, c * P:(c + 1) * P],
                                      Wh[:, s, n * NW:(n + 1) * NW], Wl[:, s, n * NW:(n + 1) * NW],
                                      k == 0, k == KT - 1)
                        if k == KT - 1 and c == 0:
                            m.then_inc(acc_half.sem, 1)
                    m.then_inc(out_used.sem, 1)

            with pe.Fori(0, DEPTH) as layer:
                turn_rows(layer, 0)
                ffn(layer, 0)
                turn_rows(layer, 1)
                mixer(layer)
                turn_rows(layer, 2)
                ffn(layer, 1)

        def landed_use(layer, f, t_use, s):
            before = 0 if f == 0 else SLOT_USES_FFN + SLOT_USES_MIX[s]
            return landed[s].sem, layer * landed[s].per_layer + (t_use * 16) + 16 * (before + 1)

        def mix_free(i):
            q = mix_occupant(i)
            if q < 0:
                return downs_done, TILES - 1 + (MIX_SLOTS[i] >= 3)
            if q == 8:
                return gates_in, 1
            if q < FIRST_ATT:
                return proj, q + 1 if q < 8 else q
            if q < FIRST_OUT:
                return att_in, 2 * [g for g, (a, n) in enumerate(ATT_GROUPS) if a <= q - FIRST_ATT][-1] + 2
            return out_used, q - FIRST_OUT + 1

        @block.scalar
        def _(act):
            def hi(s):
                return nc.scalar.activation(Wh[:, s, :], raw[:, s, :], ACT.Copy).then_inc(hi_cast.sem, 1)

            def hi_mix(layer, i):
                s = MIX_SLOTS[i]
                act.wait_ge(landed[s].sem, layer * landed[s].per_layer
                            + 16 * (SLOT_USES_FFN + MIX_SLOTS[:i].count(s) + 1))
                sig, n = mix_free(i)
                act.wait_ge(*sig.at(layer, n))
                hi(s)

            def hi_first(layer, f):
                for s in range(3):
                    act.wait_ge(*landed_use(layer, f, 0, s))
                    if f == 0:
                        act.wait_ge(*downs_done.at(layer, -1))
                    else:
                        act.wait_ge(*out_used.at(layer, 3 + s))
                    hi(s)

            def norm(layer, n):
                for c in range(HALVES):
                    act.wait_ge(*x_new.at(layer, 4 * n + 2 * c + 2))
                    nc.scalar.activation(big[:, c, :], xr[:, c, :], ACT.Square,
                                         accum_out=stat[:, c, 0:1]).then_inc(ss_done.sem, 1)
                    act.wait_ge(*ss_done.at(layer, 2 * n + c + 1))
                    nc.scalar.activation(stat[:, c, 1:2], stat[:, c, 0:1], ACT.Ln, bias=bias[:, 0:1],
                                         scale=1.0 / D_MODEL).then_inc(ln_done.sem, 1)
                    act.wait_ge(*ln_done.at(layer, 2 * n + c + 1))
                    nc.scalar.activation(stat[:, c, 2:3], stat[:, c, 1:2], ACT.Exp,
                                         scale=-0.5).then_inc(rs_done.sem, 1)

            def split_rows(layer, n):
                for c in range(HALVES):
                    for b in range(2):
                        act.wait_ge(*turned.at(layer, 4 * n + 2 * c + b + 1))
                        nc.scalar.activation(Xh[:, 4 * b:4 * b + 4, c * P:(c + 1) * P],
                                             tbank[2 * c + b][:, :].rearrange("p (k t) -> p k t", k=4),
                                             ACT.Copy).then_inc(xh_done.sem, 1)

            def step(layer, f, t, par, next_use):
                T = t + f * TILES
                s = 3 * (1 - par)

                def cast(j, used):
                    if next_use is not None:
                        act.wait_ge(*landed_use(layer, f, next_use, s + j))
                        act.wait_ge(*used.at(layer, T))
                        hi(s + j)

                act.wait_ge(*gates_done.at(layer, T + 1))
                act.wait_ge(*mul_done.at(layer, T - 1))
                nc.scalar.activation(gact[:, par, :], gbank[par][:, 0:SEQ], ACT.Silu).then_inc(silu_done.sem, 1)
                cast(0, gates_done)
                cast(1, ups_done)
                act.wait_ge(*mul_done.at(layer, T + 1))
                act.wait_ge(*downs_done.at(layer, T - 1))
                nc.scalar.activation(aH[:, par, :], hid[:, par, :], ACT.Copy).then_inc(ah_done.sem, 1)
                cast(2, downs_done)

            def ffn(layer, f):
                with act.Fori(0, TILES // 2 - 1) as g:
                    step(layer, f, g * 2, 0, g)
                    step(layer, f, g * 2 + 1, 1, g + 1)
                step(layer, f, TILES - 2, 0, TILES // 2 - 1)
                step(layer, f, TILES - 1, 1, None)

            def mixer(layer):
                act.wait_ge(*prm_set.at(layer, 1))
                pieces = ([bank[i] for i in range(8)] + [bank[1], bank[2], bank[7], bank[0]])

                def conv_dst(i):
                    return QK[:, i // 2, i % 2, :] if i < 8 else VT[:, i - 8, :]

                def conv_first(i):
                    col = R_CONV + 3 * 3 * DN_HEADS + tap_row(i)
                    act.wait_ge(*proj.at(layer, i + 1))
                    nc.scalar.activation(conv_dst(i), pieces[i][:, 0:SEQ], ACT.Copy,
                                         scale=prm[:, col:col + 1]).then_inc(conv1.sem, 1)

                def conv_silu(i):
                    act.wait_ge(*convd.at(layer, i + 1))
                    nc.scalar.activation(conv_dst(i), conv_dst(i), ACT.Silu).then_inc(conv_act.sem, 1)

                def square(h):
                    act.wait_ge(*conv_act.at(layer, 2 * h + 2))
                    if h >= 3:
                        act.wait_ge(*sumsq.at(layer, h - 2))
                    nc.scalar.activation(sq[:, h % 3, :], QK[:, h, :, :].rearrange("p a t -> p (a t)"),
                                         ACT.Square).then_inc(squared.sem, 1)

                def inverse_norm(h):
                    act.wait_ge(*sumsq.at(layer, h + 1))
                    if h >= 2:
                        act.wait_ge(*normed.at(layer, h - 1))
                    nc.scalar.activation(inv[:, h % 2, :], bank[3 + h][:, :], ACT.Ln,
                                         bias=bias[:, 0:1]).then_inc(ln2.sem, 1)
                    act.wait_ge(*ln2.at(layer, h + 1))
                    nc.scalar.activation(inv[:, h % 2, :], inv[:, h % 2, :], ACT.Exp,
                                         scale=-0.5).then_inc(inv_done.sem, 1)

                def z_silu(h):
                    act.wait_ge(*proj.at(layer, 13 + h))
                    nc.scalar.activation(SZ[:, h, :], bank[(4, 5, 2, 3)[h]][:, 0:SEQ],
                                         ACT.Silu).then_inc(z_act.sem, 1)

                for i in range(8):
                    hi_mix(layer, i + 3)
                    conv_first(i)
                    if i >= 1:
                        conv_silu(i - 1)
                        if i % 2 == 0:
                            square(i // 2 - 1)
                hi_mix(layer, 11)
                conv_silu(7)
                conv_first(8)
                hi_mix(layer, 12)
                conv_first(9)
                square(3)
                act.wait_ge(*gstep.at(layer, 4))
                nc.scalar.activation(ga[:, 3, :], ga[:, 2, :], ACT.Exp).then_inc(gexp.sem, 1)
                act.wait_ge(*gstep.at(layer, 5))
                nc.scalar.activation(ga[:, 5, 0:8], ga[:, 4, 0:8], ACT.Ln).then_inc(gln.sem, 1)
                inverse_norm(0)
                hi_mix(layer, 13)
                inverse_norm(1)
                conv_first(10)
                inverse_norm(2)
                hi_mix(layer, 14)
                inverse_norm(3)
                conv_first(11)
                act.wait_ge(*cum_read.at(layer, 1))
                nc.scalar.activation(ga[:, 17, 0:8], ga[:, 16, 0:8], ACT.Exp).then_inc(eg_done.sem, 1)
                for c in range(HALVES):
                    act.wait_ge(*diff_done.at(layer, c + 1))
                    nc.scalar.activation(dec[:, 4 * c:4 * c + 4, :], dec[:, 4 * c:4 * c + 4, :],
                                         ACT.Exp).then_inc(decayed.sem, 1)
                hi_mix(layer, 15)
                hi_mix(layer, 16)
                z_silu(0)
                z_silu(1)
                for i in range(8, 12):
                    conv_silu(i)
                hi_mix(layer, 17)
                hi_mix(layer, 18)
                z_silu(2)
                z_silu(3)
                for c in range(HALVES):
                    act.wait_ge(*v_turned.at(layer, c + 1))
                    act.wait_ge(*normed.at(layer, 4))
                    nc.scalar.activation(V[:, 4 * c:4 * c + 4, :].rearrange("p u d -> p (u d)"), bank[6 + c][:, :],
                                         ACT.Copy).then_inc(v_copied.sem, 1)
                act.wait_ge(*k_turned.at(layer, 1))
                nc.scalar.activation(Kn.rearrange("p u d -> p (u d)"), bank[0][:, :], ACT.Copy).then_inc(k_copied.sem, 1)
                for c in range(HALVES):
                    act.wait_ge(*d0_turned.at(layer, c + 1))
                    nc.scalar.activation(Dm[:, 4 * c:4 * c + 4, :].rearrange("p u d -> p (u d)"), bank[4 + c][:, :],
                                         ACT.Copy).then_inc(d_done.sem, 1)
                for i in range(19, 23):
                    hi_mix(layer, i)

                def copy_group(g):
                    first, n = ATT_GROUPS[g]
                    for c in range(HALVES):
                        j = 2 * g + c
                        act.wait_ge(*att_in.at(layer, j + 1))
                        nc.scalar.activation(big[:, c, first * P:(first + n) * P],
                                             bank[(2, 3, 1, 0, 2, 3)[j]][:, 0:n * P], ACT.Copy).then_inc(att_read.sem, 1)

                for n, s in enumerate(LEVELS):
                    for c in range(HALVES):
                        act.wait_ge(*dd_done.at(layer, 2 * n + c + 1))
                        b = bank[6 + c]
                        d = Dm[:, 4 * c:4 * c + 4, :].rearrange("p u (n a s) -> p u n a s", a=2, s=s)
                        t = DT[:, 4 * c:4 * c + 4, :].rearrange("p u (n a s) -> p u n a s", a=2, s=s)
                        if n < len(LEVELS) - 1:
                            nc.scalar.activation(d[:, :, :, 0, :], b[:, 0:256].rearrange("p (u n s) -> p u n s", u=4, s=s),
                                                 ACT.Copy).then_inc(d_done.sem, 1)
                        nc.scalar.activation(t[:, :, :, 1, :], b[:, 256:512].rearrange("p (u n s) -> p u n s", u=4, s=s),
                                             ACT.Copy).then_inc(dt_done.sem, 1)
                    if n in (0, 2, 4):
                        copy_group(n // 2)
                        for i in {0: (23, 24), 2: (25, 26), 4: (27, 28)}[n]:
                            hi_mix(layer, i)

                for j in range(2):
                    act.wait_ge(*qk_turned.at(layer, j + 1))
                    nc.scalar.activation((qT, kT)[j][:, :, :].rearrange("p a t -> p (a t)"), bank[5 + j][:, :],
                                         ACT.Copy).then_inc(qk_copied.sem, 1)
                act.wait_ge(*st_ps.at(layer, 1))
                nc.scalar.activation(St.rearrange("p u d -> p (u d)"), bank[7][:, :], ACT.Copy).then_inc(st_done.sem, 1)
                act.wait_ge(*o_ps.at(layer, 1))
                nc.scalar.activation(O[:, 0:4, :].rearrange("p u d -> p (u d)"), bank[4][:, :],
                                     ACT.Copy).then_inc(o_done.sem, 1)

                def exps(h):
                    act.wait_ge(*maxed.at(layer, h + 1))
                    p = pr[:, h % 2, :]
                    nc.scalar.activation(p[:, 0:P], p[:, 0:P], ACT.Exp, bias=mx[:, h, 0:1],
                                         accum_out=sm[:, h, 0:1]).then_inc(exped.sem, 1)
                    nc.scalar.activation(p[:, P:], p[:, P:], ACT.Exp, bias=mx[:, h, 1:2],
                                         accum_out=sm[:, h, 1:2]).then_inc(exped.sem, 1)

                def out_stats(c):
                    act.wait_ge(*o_done.at(layer, c + 1))
                    if c:
                        act.wait_ge(*o_ss.at(layer, 1))
                    nc.scalar.activation(Dsq, O[:, 4 * c:4 * c + 4, :].rearrange("p u d -> p (u d)"),
                                         ACT.Square).then_inc(o_sq.sem, 1)

                def out_inverse(c):
                    act.wait_ge(*o_var.at(layer, c + 1))
                    nc.scalar.activation(ost[:, c, 2, :], ost[:, c, 1, :], ACT.Ln).then_inc(o_ln.sem, 1)
                    act.wait_ge(*o_ln.at(layer, c + 1))
                    nc.scalar.activation(ost[:, c, 3, :], ost[:, c, 2, :], ACT.Exp, scale=-0.5).then_inc(o_rs.sem, 1)

                def copy_weights(h):
                    act.wait_ge(*pr_turned.at(layer, h + 1))
                    nc.scalar.activation(prT[:, h % 2, :], bank[7][:, 0:3 * P], ACT.Copy).then_inc(pr_copied.sem, 1)

                out_stats(0)
                exps(0)
                exps(1)
                for j in range(2):
                    act.wait_ge(*pool_ps.at(layer, j + 1))
                    nc.scalar.activation(pooled[:, j, :], bank[2 + j][:, 0:SEQ], ACT.Copy).then_inc(pool_copied.sem, 1)
                out_inverse(0)
                hi_mix(layer, 29)
                for j in range(2):
                    act.wait_ge(*pool_out.at(layer, j + 1))
                    nc.scalar.activation(Xh[:, 2 + j, :], bank[2 + j][:, 0:SEQ], ACT.Copy,
                                         scale=prm[:, R_PSCALE + j:R_PSCALE + j + 1]).then_inc(pool_hi.sem, 1)
                hi_mix(layer, 30)
                out_stats(1)
                out_inverse(1)
                copy_weights(0)
                copy_weights(1)
                exps(2)
                act.wait_ge(*att_out.at(layer, 1))
                nc.scalar.activation(Xh[:, 0, :], bank[4][:, 0:SEQ], ACT.Copy).then_inc(att_hi.sem, 1)
                exps(3)
                copy_weights(2)
                copy_weights(3)
                act.wait_ge(*att_out.at(layer, 2))
                nc.scalar.activation(Xh[:, 1, :], bank[5][:, 0:SEQ], ACT.Copy).then_inc(att_hi.sem, 1)
                for c in range(HALVES):
                    act.wait_ge(*y_gated.at(layer, c + 1))
                    nc.scalar.activation(Xh[:, 4:8, c * P:(c + 1) * P], Yf[:, 4 * c:4 * c + 4, :],
                                         ACT.Copy).then_inc(y_hi.sem, 1)
                hi_mix(layer, 31)
                hi_mix(layer, 32)

            act.dma_start(pos_i[:, :], positions[0].rearrange("(c p) -> p c", p=P),
                          allow_slow_non_contiguous=True).then_inc(small_in.sem, 16)
            act.dma_start(prm_rows[0:R_PSCALE, :, :],
                          dn_conv_w.rearrange("l t (r c) -> (t r) l c", c=P)).then_inc(rows_in.sem, 16)
            act.dma_start(prm_rows[R_PSCALE:R_ONORM, :, :],
                          pool_scale.rearrange("l (r c) -> r l c", c=P)).then_inc(rows_in.sem, 16)
            act.dma_start(prm_rows[R_ONORM:R_END, :, :],
                          dn_out_norm.rearrange("(a l) c -> a l c", a=1)).then_inc(rows_in.sem, 16)
            act.dma_start(dt_all[:, :, :].rearrange("p l h -> p (l h)"),
                          dn_dt_bias.rearrange("l h -> (l h)").partition_broadcast(P)).then_inc(small_in.sem, 16)
            act.dma_start(al_all[:, :, :].rearrange("p l h -> p (l h)"),
                          dn_a_log.rearrange("l h -> (l h)").partition_broadcast(P)).then_inc(small_in.sem, 16)
            for l in range(DEPTH):
                for a in range(2):
                    act.dma_start(pw[a * POOL_DIM:(a + 1) * POOL_DIM, l, :, :],
                                  pool_w[l].rearrange("(j a) c d -> a c j d", a=2)[a]).then_inc(small_in.sem, 16)
            act.dma_start(cst[:, C_FIRST:], consts[:, C_FIRST:]).then_inc(masks_in.sem, 16)
            act.wait_ge(*trig.at(0, 1))
            nc.scalar.activation(sind[:, :, :].rearrange("p c e -> p (c e)"), ang[:, 3, :], ACT.Sin).then_inc(prologue.sem, 1)
            nc.scalar.activation(cosd[:, :, :].rearrange("p c e -> p (c e)"), ang[:, 5, :], ACT.Sin).then_inc(prologue.sem, 1)
            act.wait_ge(small_in.sem, 16 * (2 * DEPTH + 3))
            nc.scalar.activation(al_all[:, :, :], al_all[:, :, :], ACT.Exp).then_inc(prologue.sem, 1)

            with act.Fori(0, DEPTH) as layer:
                hi_first(layer, 0)
                norm(layer, 0)
                split_rows(layer, 0)
                ffn(layer, 0)
                for i in range(3):
                    hi_mix(layer, i)
                norm(layer, 1)
                split_rows(layer, 1)
                mixer(layer)
                hi_first(layer, 1)
                norm(layer, 2)
                split_rows(layer, 2)
                ffn(layer, 1)
            norm(DEPTH, 0)

        @block.vector
        def _(dve):
            def lo(s):
                return nc.vector.tensor_tensor(Wl[:, s, :], raw[:, s, :], Wh[:, s, :].bitcast(F32),
                                               ALU.subtract).then_inc(lo_cast.sem, 1)

            def lo_piece(layer, index, s):
                dve.wait_ge(*hi_cast.at(layer, index + 1))
                lo(s)

            def lo_mix(layer, i):
                lo_piece(layer, MIX_BASE + i, MIX_SLOTS[i])

            def inverse_rms(layer, n, c, weight_loads):
                m = 4 * (2 * n + c)
                st = [stat[:, c, i:i + 1] for i in range(8)]
                dve.wait_ge(*ss_done.at(layer, 2 * n + c + 1))
                nc.vector.tensor_scalar(st[3], st[0], 1.0 / D_MODEL, EPS, ALU.mult, ALU.add).then_inc(newton.sem, 1)
                dve.wait_ge(*newton.at(layer, m + 1))
                dve.wait_ge(*rs_done.at(layer, 2 * n + c + 1))
                nc.vector.scalar_tensor_tensor(st[4], st[3], st[2], st[2], ALU.mult, ALU.mult).then_inc(newton.sem, 1)
                dve.wait_ge(*newton.at(layer, m + 2))
                nc.vector.tensor_scalar(st[5], st[4], -0.5, 1.5, ALU.mult, ALU.add).then_inc(newton.sem, 1)
                dve.wait_ge(*newton.at(layer, m + 3))
                nc.vector.tensor_tensor(st[6], st[5], st[2], ALU.mult).then_inc(newton.sem, 1)
                dve.wait_ge(*newton.at(layer, m + 4))
                dve.wait_ge(*norm_w_in.at(layer, 16 * (n + 1)))
                return nc.vector.scalar_tensor_tensor(big[:, c, :], xr[:, c, :], st[6], norm_w[:, :],
                                                      ALU.mult, ALU.mult)

            def norm(layer, n):
                for c in range(HALVES):
                    inverse_rms(layer, n, c, None).then_inc(rows_normed.sem, 1)

            def split_rows(layer, n):
                for c in range(HALVES):
                    for b in range(2):
                        dve.wait_ge(*xh_done.at(layer, 4 * n + 2 * c + b + 1))
                        t = slice(c * P, (c + 1) * P)
                        nc.vector.tensor_tensor(Xl[:, 4 * b:4 * b + 4, t],
                                                tbank[2 * c + b][:, :].rearrange("p (k t) -> p k t", k=4),
                                                Xh[:, 4 * b:4 * b + 4, t].bitcast(F32), ALU.subtract).then_inc(xl_done.sem, 1)

            def step(layer, f, t, par, cast_next):
                T = t + f * TILES
                s = 3 * (1 - par)

                def cast(j):
                    if cast_next:
                        dve.wait_ge(*hi_cast.at(layer, t * 3 + (FFN_BASE[f] + 3 + j + 1)))
                        lo(s + j)

                cast(0)
                dve.wait_ge(*silu_done.at(layer, T + 1))
                dve.wait_ge(*ups_done.at(layer, T + 1))
                nc.vector.tensor_tensor(hid[:, par, :], ubank[par][:, 0:SEQ], gact[:, par, :],
                                        ALU.mult).then_inc(mul_done.sem, 1)
                cast(1)
                dve.wait_ge(*ah_done.at(layer, T + 1))
                nc.vector.tensor_tensor(aL[:, par, :], hid[:, par, :], aH[:, par, :].bitcast(F32),
                                        ALU.subtract).then_inc(al_done.sem, 1)
                cast(2)

            def ffn(layer, f):
                with dve.Fori(0, TILES // 2 - 1) as g:
                    step(layer, f, g * 2, 0, True)
                    step(layer, f, g * 2 + 1, 1, True)
                step(layer, f, TILES - 2, 0, True)
                step(layer, f, TILES - 1, 1, False)

            def update(layer, part, scale, done):
                for c in range(HALVES):
                    if c == 0:
                        dve.wait_ge(*acc_half.at(layer, part + 1))
                    else:
                        dve.wait_ge(*done)
                    for n in range(2):
                        r = xr[:, c, n * NW:(n + 1) * NW]
                        nc.vector.scalar_tensor_tensor(r, acc[c][n][:, :], scale, r, ALU.mult,
                                                       ALU.add).then_inc(x_new.sem, 1)

            def mixer(layer):
                def conv_rest(i):
                    src = ([bank[b] for b in range(8)] + [bank[1], bank[2], bank[7], bank[0]])[i]
                    dst = QK[:, i // 2, i % 2, :] if i < 8 else VT[:, i - 8, :]
                    dve.wait_ge(*conv1.at(layer, i + 1))
                    for back in range(1, TAPS):
                        col = R_CONV + (TAPS - 1 - back) * 3 * DN_HEADS + tap_row(i)
                        op = nc.vector.scalar_tensor_tensor(dst[:, back:], src[:, 0:SEQ - back], prm[:, col:col + 1],
                                                            dst[:, back:], ALU.mult, ALU.add)
                        if back < TAPS - 1:
                            op.then_inc(conv_mid.sem, 1)
                            dve.wait_ge(*conv_mid.at(layer, 2 * i + back))
                        else:
                            op.then_inc(convd.sem, 1)

                count = [0]

                def small(op):
                    count[0] += 1
                    op.then_inc(gstep.sem, 1)
                    dve.wait_ge(*gstep.at(layer, count[0]))

                gin = ga[:, 0, :].rearrange("p (c e) -> p c e", c=2)
                gneg = ga[:, 2, :].rearrange("p (c e) -> p c e", c=2)
                gex = ga[:, 3, :].rearrange("p (c e) -> p c e", c=2)

                def row(n):
                    return ga[:, n, 0:8].rearrange("p (c e) -> p c e", c=2)

                def per_head(n):
                    return ga[:, n, 0:4].unsqueeze(1).broadcast_to([P, 2, 4])

                for i in range(8):
                    lo_mix(layer, i + 3)
                    conv_rest(i)
                lo_mix(layer, 11)
                dve.wait_ge(*gates_in.at(layer, 1))
                small(nc.vector.tensor_copy(ga[:, 0, :], bank[0][:, 0:16]))
                small(nc.vector.tensor_tensor(row(1), gin[:, :, 4:8], per_head(14), ALU.add))
                small(nc.vector.tensor_scalar(gneg[:, :, 0:4], gin[:, :, 0:4], -1.0, 87.0, ALU.mult, ALU.min))
                small(nc.vector.scalar_tensor_tensor(gneg[:, :, 4:8], row(1), -1.0, row(1), ALU.mult, ALU.min))
                conv_rest(8)
                lo_mix(layer, 12)
                dve.wait_ge(*gexp.at(layer, 1))
                e = gex[:, :, 4:8]
                small(nc.vector.tensor_scalar(row(4), e, 1.0, None, ALU.add))
                small(nc.vector.tensor_scalar(row(6), gex[:, :, 0:4], 1.0, None, ALU.add))
                small(nc.vector.reciprocal(ga[:, 7, 0:8], ga[:, 6, 0:8]))
                small(nc.vector.tensor_scalar(row(8), row(4), -1.0, 1e-30, ALU.add, ALU.max))
                small(nc.vector.reciprocal(ga[:, 10, 0:8], ga[:, 8, 0:8]))
                small(nc.vector.tensor_tensor(row(11), row(10), e, ALU.mult))
                small(nc.vector.tensor_scalar(row(12), e, -0.5, 1.0, ALU.mult, ALU.add))
                small(nc.vector.tensor_tensor(row(13), row(12), e, ALU.mult))
                dve.wait_ge(*gln.at(layer, 1))
                small(nc.vector.tensor_tensor(ga[:, 11, 0:8], ga[:, 11, 0:8], ga[:, 5, 0:8], ALU.mult))
                small(nc.vector.tensor_tensor(ga[:, 11, 0:8], ga[:, 11, 0:8], ga[:, 13, 0:8], ALU.max))
                small(nc.vector.scalar_tensor_tensor(ga[:, 1, 0:8], ga[:, 1, 0:8], 0.0, ga[:, 11, 0:8], ALU.max, ALU.add))
                small(nc.vector.tensor_tensor(row(9), row(1), per_head(15), ALU.mult))
                beta, gc, eg, neg_e = ga[:, 7, :], ga[:, 16, :], ga[:, 17, :], ga[:, 18, :]
                nc.vector.tensor_tensor(grow[:, :, :], tri.unsqueeze(1).broadcast_to([P, UNITS, P]),
                                        ga[:, 9, 0:8].unsqueeze(2).broadcast_to([P, UNITS, P]),
                                        ALU.mult).then_inc(tri_g.sem, 1)
                conv_rest(9)

                def l2norm(h):
                    dve.wait_ge(*inv_done.at(layer, h + 1))
                    q, k = QK[:, h, 0, :], QK[:, h, 1, :]
                    nc.vector.scalar_tensor_tensor(q, q, DN_SCALE, inv[:, h % 2, 0:SEQ], ALU.mult, ALU.mult)
                    nc.vector.tensor_tensor(k, k, inv[:, h % 2, SEQ:], ALU.mult).then_inc(normed.sem, 1)

                l2norm(0)
                lo_mix(layer, 13)
                l2norm(1)
                conv_rest(10)
                l2norm(2)
                lo_mix(layer, 14)
                l2norm(3)
                conv_rest(11)
                dve.wait_ge(*cum_col.at(layer, 1))
                nc.vector.tensor_copy(gc[:, 0:8], bank[1][:, 0:8]).then_inc(cum_read.sem, 1)
                dve.wait_ge(*cum_read.at(layer, 1))
                for c in range(HALVES):
                    dve.wait_ge(*cum_row.at(layer, c + 1))
                    for h in range(DN_HEADS):
                        u = 4 * c + h
                        op = nc.vector.scalar_tensor_tensor(dec[:, u, :], bank[2 + c][:, h * P:(h + 1) * P], gc[:, u:u + 1],
                                                            neg, ALU.subtract, ALU.add)
                    op.then_inc(diff_done.sem, 1)
                dve.wait_ge(*eg_done.at(layer, 1))
                nc.vector.tensor_scalar(neg_e[:, 0:8], eg[:, 0:8], -1.0, None, ALU.mult).then_inc(neg_eg.sem, 1)

                def unit_gram(n):
                    c = n // 2
                    dve.wait_ge(*gram.at(layer, n + 1))
                    dve.wait_ge(*decayed.at(layer, c + 1))
                    b = bank[(6, 7, 0, 1)[n]][:, :].rearrange("p (u a t) -> p u a t", u=2, a=2)
                    for j in range(2):
                        u = 2 * n + j
                        op = nc.vector.scalar_tensor_tensor(LT[:, u, :], b[:, j, 1, :], beta[:, u:u + 1], dec[:, u, :],
                                                            ALU.mult, ALU.mult)
                    op.then_inc(lt_raw.sem, 1)
                    nc.vector.tensor_tensor(aT[:, 2 * n:2 * n + 2, :], b[:, :, 0, :], dec[:, 2 * n:2 * n + 2, :],
                                            ALU.mult).then_inc(at_done.sem, 1)

                for n in range(4):
                    unit_gram(n)
                lo_mix(layer, 15)
                for c in range(HALVES):
                    dve.wait_ge(*lt_done.at(layer, c + 1))
                    pair = cst[:, C_PAIR:C_PAIR + P].unsqueeze(1).broadcast_to([P, 4, P])
                    nc.vector.tensor_tensor(DT[:, 4 * c:4 * c + 4, :], LT[:, 4 * c:4 * c + 4, :], pair,
                                            ALU.mult).then_inc(dt0_done.sem, 1)
                for i in range(16, 23):
                    lo_mix(layer, i)
                for n in range(len(LEVELS)):
                    mask = cst[:, C_LEVEL + n * P:C_LEVEL + (n + 1) * P].unsqueeze(1).broadcast_to([P, 4, P])
                    for c in range(HALVES):
                        dve.wait_ge(*p_done.at(layer, 2 * n + c + 1))
                        nc.vector.tensor_tensor(PM[:, 4 * c:4 * c + 4, :],
                                                bank[4 + c][:, :].rearrange("p (u t) -> p u t", u=4), mask,
                                                ALU.mult).then_inc(pm_done.sem, 1)
                    if n in (0, 2, 4):
                        for i in {0: (23, 24), 2: (25, 26), 4: (27, 28)}[n]:
                            lo_mix(layer, i)

                def new_values(c):
                    u = slice(4 * c, 4 * c + 4)
                    dve.wait_ge(*vn_ps.at(layer, c + 1))
                    nc.vector.tensor_tensor(Vn[:, u, :], bank[(4, 7)[c]][:, :].rearrange("p (u d) -> p u d", u=4),
                                            beta[:, u].unsqueeze(2).broadcast_to([P, 4, P]), ALU.mult).then_inc(vn_done.sem, 1)

                new_values(0)
                dve.wait_ge(*vn_done.at(layer, 1))
                nc.vector.tensor_tensor(Vd, Vn[:, 0:4, :], dec[:, 0:4, P - 1:P].broadcast_to([P, 4, P]),
                                        ALU.mult).then_inc(vd_done.sem, 1)
                dve.wait_ge(*ks_ps.at(layer, 1))
                dve.wait_ge(*neg_eg.at(layer, 1))
                for h in range(DN_HEADS):
                    op = nc.vector.scalar_tensor_tensor(R1[:, h, :], bank[5][:, h * P:(h + 1) * P], neg_e[:, 4 + h:5 + h],
                                                        V[:, 4 + h, :], ALU.mult, ALU.add)
                op.then_inc(r1_done.sem, 1)
                dve.wait_ge(*qs_ps.at(layer, 1))
                nc.vector.tensor_tensor(QS, bank[6][:, :].rearrange("p (u d) -> p u d", u=4),
                                        eg[:, 4:8].unsqueeze(2).broadcast_to([P, 4, P]), ALU.mult).then_inc(qs_done.sem, 1)

                def mask_scores(h):
                    dve.wait_ge(*scored.at(layer, h + 1))
                    if h >= 2:
                        dve.wait_ge(*pr_turned.at(layer, h - 1))
                    p = pr[:, h % 2, :]
                    nc.vector.scalar_tensor_tensor(p, bank[h % 2][:, 0:3 * P], ATT_SCALE, att_mask, ALU.mult,
                                                   ALU.add).then_inc(masked.sem, 1)
                    dve.wait_ge(*masked.at(layer, h + 1))
                    nc.vector.tensor_reduce(mx[:, h, 0:1], p[:, 0:P], AX.X, ALU.max, negate=True)
                    nc.vector.tensor_reduce(mx[:, h, 1:2], p[:, P:], AX.X, ALU.max, negate=True).then_inc(maxed.sem, 1)

                def weigh(h):
                    dve.wait_ge(*exped.at(layer, 2 * h + 2))
                    nc.vector.reciprocal(rc[:, h, :], sm[:, h, :]).then_inc(recip.sem, 1)
                    dve.wait_ge(*recip.at(layer, h + 1))
                    p = pr[:, h % 2, :]
                    nc.vector.tensor_scalar(p[:, 0:P], p[:, 0:P], rc[:, h, 0:1], None, ALU.mult)
                    nc.vector.tensor_scalar(p[:, P:], p[:, P:], rc[:, h, 1:2], None, ALU.mult).then_inc(weighted.sem, 1)

                def out_variance(c):
                    dve.wait_ge(*o_sq.at(layer, c + 1))
                    nc.vector.tensor_reduce(ost[:, c, 0, :], Dsq.rearrange("p (u d) -> p u d", u=4), AX.X,
                                            ALU.add).then_inc(o_ss.sem, 1)
                    dve.wait_ge(*o_ss.at(layer, c + 1))
                    nc.vector.tensor_scalar(ost[:, c, 1, :], ost[:, c, 0, :], 1.0 / P, EPS, ALU.mult,
                                            ALU.add).then_inc(o_var.sem, 1)

                def out_norm(c):
                    dve.wait_ge(*o_rs.at(layer, c + 1))
                    s = [ost[:, c, i, :] for i in range(8)]
                    nc.vector.tensor_tensor(s[4], s[3], s[3], ALU.mult).then_inc(o_newton.sem, 1)
                    dve.wait_ge(*o_newton.at(layer, 3 * c + 1))
                    nc.vector.tensor_tensor(s[5], s[4], s[1], ALU.mult).then_inc(o_newton.sem, 1)
                    dve.wait_ge(*o_newton.at(layer, 3 * c + 2))
                    nc.vector.tensor_scalar(s[6], s[5], -0.5, 1.5, ALU.mult, ALU.add).then_inc(o_newton.sem, 1)
                    dve.wait_ge(*o_newton.at(layer, 3 * c + 3))
                    nc.vector.tensor_tensor(s[7], s[6], s[3], ALU.mult).then_inc(o_newton2.sem, 1)
                    dve.wait_ge(*o_newton2.at(layer, c + 1))
                    o = O[:, 4 * c:4 * c + 4, :]
                    nc.vector.tensor_tensor(o, o, s[7].unsqueeze(2).broadcast_to([P, 4, P]),
                                            ALU.mult).then_inc(o_normed.sem, 1)

                mask_scores(0)
                out_variance(0)
                mask_scores(1)
                new_values(1)
                weigh(0)
                out_norm(0)
                weigh(1)
                dve.wait_ge(*o_ps.at(layer, 2))
                nc.vector.tensor_tensor(O[:, 4:8, :], bank[6][:, :].rearrange("p (u d) -> p u d", u=4), QS,
                                        ALU.add).then_inc(o_done.sem, 1)
                lo_mix(layer, 29)
                for j in range(2):
                    dve.wait_ge(*pool_hi.at(layer, j + 1))
                    nc.vector.scalar_tensor_tensor(Xl[:, 2 + j, :], bank[2 + j][:, 0:SEQ],
                                                   prm[:, R_PSCALE + j:R_PSCALE + j + 1],
                                                   Xh[:, 2 + j, :].bitcast(F32), ALU.mult, ALU.subtract).then_inc(pool_lo.sem, 1)
                lo_mix(layer, 30)
                out_variance(1)
                mask_scores(2)
                mask_scores(3)
                out_norm(1)
                weigh(2)
                dve.wait_ge(*att_hi.at(layer, 1))
                nc.vector.tensor_tensor(Xl[:, 0, :], bank[4][:, 0:SEQ], Xh[:, 0, :].bitcast(F32),
                                        ALU.subtract).then_inc(att_lo.sem, 1)
                weigh(3)
                dve.wait_ge(*att_hi.at(layer, 2))
                nc.vector.tensor_tensor(Xl[:, 1, :], bank[5][:, 0:SEQ], Xh[:, 1, :].bitcast(F32),
                                        ALU.subtract).then_inc(att_lo.sem, 1)
                for c in range(HALVES):
                    u = slice(4 * c, 4 * c + 4)
                    dve.wait_ge(*o_turned.at(layer, c + 1))
                    nc.vector.scalar_tensor_tensor(Yf[:, u, :], bank[6 + c][:, :].rearrange("p (u d) -> p u d", u=4),
                                                   prm[:, R_ONORM:R_ONORM + 1], SZ[:, :, c * P:(c + 1) * P],
                                                   ALU.mult, ALU.mult).then_inc(y_gated.sem, 1)
                for c in range(HALVES):
                    dve.wait_ge(*y_hi.at(layer, c + 1))
                    nc.vector.tensor_tensor(Xl[:, 4:8, c * P:(c + 1) * P], Yf[:, 4 * c:4 * c + 4, :],
                                            Xh[:, 4:8, c * P:(c + 1) * P].bitcast(F32), ALU.subtract).then_inc(y_lo.sem, 1)
                lo_mix(layer, 31)
                lo_mix(layer, 32)

            for s, n in ((lo_cast, SLOTS), (silu_done, 2), (mul_done, 2), (ah_done, 2), (al_done, 2), (rows_normed, 2)):
                dve.sem_inc(s.sem, n)
            nc.vector.memset(bias[:, 0:1], EPS).then_inc(zeroed.sem, 1)
            nc.vector.memset(bias[:, 1:2], 1.0).then_inc(zeroed.sem, 1)
            dve.wait_ge(small_in.sem, 16 * (2 * DEPTH + 3))
            dve.wait_ge(consts_in.sem, 16)
            n_pro = [0]

            def pro(op):
                n_pro[0] += 1
                op.then_inc(pro_step.sem, 1)
                dve.wait_ge(pro_step.sem, n_pro[0])

            pro(nc.vector.tensor_copy(pos_f[:, :], pos_i[:, :]))
            half = ATT_DIM // 2
            freq = cst[:, C_FREQ:C_FREQ + half].unsqueeze(1).broadcast_to([P, 2, half])
            for c in range(HALVES):
                th = ang[:, 0, c * ATT_DIM:(c + 1) * ATT_DIM].rearrange("p (a e) -> p a e", a=2)
                pro(nc.vector.tensor_scalar(th, freq, pos_f[:, c:c + 1], None, ALU.mult))
            TURN = 2 * np.pi
            parts = [6.28125, 0.0, 0.0]
            parts[1] = float(np.round((TURN - parts[0]) * 2 ** 20) / 2 ** 20)
            parts[2] = TURN - parts[0] - parts[1]
            rounder = 1.5 * 2 ** 23
            for quarter, at in ((0.0, 3), (0.25, 5)):
                pro(nc.vector.tensor_scalar(ang[:, 1, :], ang[:, 0, :], 1.0 / TURN, quarter, ALU.mult, ALU.add))
                pro(nc.vector.tensor_scalar(ang[:, 1, :], ang[:, 1, :], rounder, None, ALU.add))
                pro(nc.vector.tensor_scalar(ang[:, 1, :], ang[:, 1, :], -rounder, None, ALU.add))
                pro(nc.vector.scalar_tensor_tensor(ang[:, 2, :], ang[:, 1, :], -parts[0], ang[:, 0, :], ALU.mult, ALU.add))
                pro(nc.vector.scalar_tensor_tensor(ang[:, 2, :], ang[:, 1, :], -parts[1], ang[:, 2, :], ALU.mult, ALU.add))
                pro(nc.vector.scalar_tensor_tensor(ang[:, 2, :], ang[:, 1, :], -parts[2], ang[:, 2, :], ALU.mult, ALU.add))
                pro(nc.vector.tensor_scalar(ang[:, at - 1, :] if at == 5 else ang[:, 2, :], ang[:, 2, :],
                                            quarter * TURN, None, ALU.add))
                pro(nc.vector.tensor_scalar(ang[:, at, :], ang[:, at - 1, :] if at == 5 else ang[:, 2, :],
                                            3.1415925, -3.1415925, ALU.min, ALU.max))
            pro(nc.vector.tensor_copy(pos_f[:, 0:1], ang[:, 5, 0:1]))
            nc.vector.tensor_copy(pos_f[:, 1:2], ang[:, 3, 0:1]).then_inc(trig.sem, 1)
            dve.wait_ge(prm_turned.sem, DEPTH)
            pro(nc.vector.tensor_copy(prm_all[:, :, :], bank[0][:, 0:DEPTH * P]
                                      .rearrange("p (l r) -> p l r", l=DEPTH)[:, :, 0:R_END]))
            dve.wait_ge(prologue.sem, 3)
            pro(nc.vector.tensor_scalar(al_all[:, :, :], al_all[:, :, :], -1.0, None, ALU.mult))
            dve.wait_ge(zeroed.sem, 2)
            dve.wait_ge(masks_in.sem, 16)
            for c in range(HALVES):
                dve.wait_ge(x_in[c].sem, 16)
                dve.sem_inc(x_new.sem, 2)

            with dve.Fori(0, DEPTH) as layer:
                nc.vector.tensor_copy(prm[:, :], prm_all[:, bass.ds(layer, 1), :].squeeze(1))
                nc.vector.tensor_copy(pwl[:, :, :].rearrange("p j d -> p (j d)"),
                                      pw[:, bass.ds(layer, 1), :, :].squeeze(1).rearrange("p j d -> p (j d)"))
                nc.vector.tensor_copy(ga[:, 14, 0:4], dt_all[:, bass.ds(layer, 1), :].squeeze(1))
                nc.vector.tensor_copy(ga[:, 15, 0:4], al_all[:, bass.ds(layer, 1), :].squeeze(1)).then_inc(prm_set.sem, 1)
                dve.wait_ge(*prm_set.at(layer, 1))
                lo_piece(layer, 0, 0)
                norm(layer, 0)
                lo_piece(layer, 1, 1)
                split_rows(layer, 0)
                lo_piece(layer, 2, 2)
                ffn(layer, 0)
                for i in range(3):
                    lo_mix(layer, i)
                update(layer, 0, 0.5, downs_done.at(layer, TILES))
                norm(layer, 1)
                split_rows(layer, 1)
                mixer(layer)
                for j in range(3):
                    lo_piece(layer, FFN_BASE[1] + j, j)
                update(layer, 1, 1.0, out_used.at(layer, OUT_PIECES))
                norm(layer, 2)
                split_rows(layer, 2)
                ffn(layer, 1)
                update(layer, 2, 0.5, downs_done.at(layer, 2 * TILES))
            for c in range(HALVES):
                inverse_rms(DEPTH, 0, c, None).then_inc(out_ready.sem, 1)


_INS = ("x", "positions", "ffn1_norm", "ffn1_w_gate", "ffn1_w_up", "ffn1_w_down", "mix_norm", "w_in", "pool_w",
        "pool_scale", "dn_conv_w", "dn_a_log", "dn_dt_bias", "dn_out_norm", "w_out", "ffn2_norm", "ffn2_w_gate",
        "ffn2_w_up", "ffn2_w_down", "final_norm")


def kernel(**inputs):
    import concourse.bacc as bacc
    from concourse.bass_utils import run_bass_kernel_spmd

    nc = bacc.Bacc("TRN2", target_bir_lowering=False, num_devices=1)
    arrays = {n: np.ascontiguousarray(inputs[n]) for n in _INS}
    arrays["consts"] = constants()
    args = {n: nc.dram_tensor(f"in_{n}", a.shape, mybir.dt.from_np(a.dtype), kind="ExternalInput").ap()
            for n, a in arrays.items()}
    args["out"] = nc.dram_tensor("out_x", (1, SEQ, D_MODEL), F32, kind="ExternalOutput").ap()
    build(nc, **args)
    r = run_bass_kernel_spmd(nc, [{f"in_{n}": a for n, a in arrays.items()}], core_ids=[0])
    return r.results[0]["out_x"]
```

```python
import math
from contextlib import ExitStack

import numpy as np

import concourse.bass as bass
from concourse import mybir

F32 = mybir.dt.float32
F32R = mybir.dt.float32r
I32 = mybir.dt.int32
ALU = mybir.AluOpType
ACT = mybir.ActivationFunctionType
AX = mybir.AxisListType

P = 128
D_MODEL = 1024
SEQ = 256
DEPTH = 2
D_FF = 2816
EPS = 1e-6
HALVES = SEQ // P
KT = D_MODEL // P
TILES = D_FF // P
NW = 512

ATT_HEADS, ATT_DIM = 4, 64
ATT_SCALE = ATT_DIM ** -0.5
PATTERNS = ((128, 1), (512, 4), (2048, 16))
POOL_WINDOWS = (2, 4, 8, 16)
POOL_DIM = 64
DN_HEADS = 4
DN_SCALE = 128 ** -0.5
TAPS = 4
UNITS = HALVES * DN_HEADS
ROPE_THETA = 10000.0

COL_AQ, COL_DQ, COL_DK, COL_DV, COL_DZ, IN_WIDTH = 0, 1024, 1536, 2048, 2560, 3080
GATES = 2 * DN_HEADS

SLOTS = 6
IN_PIECES = ([("qk", h, j) for h in range(DN_HEADS) for j in range(2)] + [("gates", 0, 0)]
             + [("v", h, 0) for h in range(DN_HEADS)] + [("z", h, 0) for h in range(DN_HEADS)])
N_IN_B = len(IN_PIECES)
ATT_PIECES = 2 * ATT_HEADS * ATT_DIM * 2 // P
ATT_GROUPS = [(0, 3), (3, 3), (6, 2)]
OUT_PIECES = KT
OUT_ORDER = (2, 3, 0, 1, 4, 5, 6, 7)
LEVEL_CASTS = ((20, 21), (22,), (23, 24), (25,), (26, 27), (28,))
MIX_SLOTS = ([i % SLOTS for i in range(N_IN_B)] + [i % SLOTS for i in range(ATT_PIECES)]
             + [2, 3, 4, 5, 0, 1, 3, 4])
assert len(MIX_SLOTS) == N_IN_B + ATT_PIECES + OUT_PIECES
FIRST_ATT = N_IN_B
FIRST_OUT = N_IN_B + ATT_PIECES
MIX_PIECES = len(MIX_SLOTS)
FFN_PIECES = 3 * TILES
LAYER_PIECES = 2 * FFN_PIECES + MIX_PIECES
MIX_BASE = FFN_PIECES
FFN_BASE = (0, FFN_PIECES + MIX_PIECES)
SLOT_USES_MIX = [MIX_SLOTS.count(s) for s in range(SLOTS)]
SLOT_USES_FFN = TILES // 2
SLOT_USES = [2 * SLOT_USES_FFN + n for n in SLOT_USES_MIX]


def tap_row(i):
    return (i % 2) * DN_HEADS + i // 2 if i < 2 * DN_HEADS else i


def mix_occupant(i):
    for q in range(i - 1, -1, -1):
        if MIX_SLOTS[q] == MIX_SLOTS[i]:
            return q
    return -1


LN_EXP, SILU = "natural_log_exp_and_others", "silu_and_others"
LEVELS = (2, 4, 8, 16, 32, 64)

C_IDENT = 0
C_FREQ = C_IDENT + P
C_FIRST = C_FREQ + ATT_DIM // 2
C_TRI = C_FIRST
C_NEG = C_TRI + P
C_PAIR = C_NEG + P
C_LEVEL = C_PAIR + P
C_ONES = C_LEVEL + P * len(LEVELS)
C_ATT = C_ONES + P
C_POOL = C_ATT + 3 * P
C_END = C_POOL + len(POOL_WINDOWS) * (SEQ + P)

R_CONV = 0
R_PSCALE = R_CONV + TAPS * 3 * DN_HEADS
R_ONORM = R_PSCALE + 2
R_END = R_ONORM + 1


def constants():
    c = np.zeros((P, C_END), np.float32)
    r, k = np.arange(P)[:, None], np.arange(P)[None, :]
    c[:, C_IDENT:C_IDENT + P] = r == k
    c[:, C_TRI:C_TRI + P] = r <= k
    c[:, C_NEG:C_NEG + P] = np.where(r <= k, 0.0, -1e30)
    c[:, C_PAIR:C_PAIR + P] = np.where(r == k, 1.0, np.where((r % 2 == 0) & (k == r + 1), -1.0, 0.0))
    for n, s in enumerate(LEVELS):
        below = ((r // s) % 2 == 1) & (k // s == r // s - 1)
        c[:, C_LEVEL + n * P:C_LEVEL + (n + 1) * P] = np.where(r == k, 1.0, np.where(below, -1.0, 0.0))
    c[:, C_ONES:C_ONES + P] = 1.0
    for n, away in enumerate((0, P, 0)):
        d = away + r - k
        count = np.zeros_like(d)
        for window, dilation in PATTERNS:
            count = count + ((d >= 0) & (d <= window) & (d % dilation == 0))
        c[:, C_ATT + n * P:C_ATT + (n + 1) * P] = np.where(count > 0, np.log(np.maximum(count, 1)), -1e30)
    for g, w in enumerate(POOL_WINDOWS):
        s, t = np.arange(SEQ)[:, None], np.arange(SEQ)[None, :]
        m = np.where((t >= s) & (t - s < w), 1.0 / np.minimum(t + 1, w), 0.0) - (s == t)
        at = C_POOL + g * (SEQ + P)
        c[:, at:at + SEQ] = m[:P]
        c[:, at + SEQ:at + SEQ + P] = m[P:, P:]
    half = ATT_DIM // 2
    c[:, C_FREQ:C_FREQ + half] = (np.float32(ROPE_THETA) ** (-np.arange(0, ATT_DIM, 2, dtype=np.float32)
                                                             / np.float32(ATT_DIM)))[None, :]
    return c


class Signal:

    def __init__(self, sem, per_layer, start=0):
        self.sem, self.per_layer, self.start = sem, per_layer, start

    def at(self, layer, n):
        return self.sem, layer * self.per_layer + n + self.start


def build(nc, x, positions, ffn1_norm, ffn1_w_gate, ffn1_w_up, ffn1_w_down, mix_norm, w_in, pool_w,
          pool_scale, dn_conv_w, dn_a_log, dn_dt_bias, dn_out_norm, w_out, ffn2_norm, ffn2_w_gate,
          ffn2_w_up, ffn2_w_down, final_norm, consts, out):
    ctx = ExitStack()
    with ctx:
        def sb(name, shape, dt=F32):
            return ctx.enter_context(nc.sbuf_tensor(name, shape, dt))

        def signal(name, per_layer=0, start=0):
            return Signal(ctx.enter_context(nc.semaphore(name)), per_layer, start)

        cst = sb("cst", [P, C_END])
        xr = sb("xr", [P, HALVES, D_MODEL])
        Xh = sb("Xh", [P, KT, SEQ], F32R)
        Xl = sb("Xl", [P, KT, SEQ], F32R)
        raw = sb("raw", [P, SLOTS, D_MODEL])
        Wh = sb("Wh", [P, SLOTS, D_MODEL], F32R)
        Wl = sb("Wl", [P, SLOTS, D_MODEL], F32R)
        aH = sb("aH", [P, 2, SEQ], F32R)
        aL = sb("aL", [P, 2, SEQ], F32R)
        gact = sb("gact", [P, 2, SEQ])
        hid = sb("hid", [P, 2, SEQ])
        norm_w = sb("norm_w", [P, D_MODEL])
        stat = sb("stat", [P, HALVES, 8])
        bias = sb("bias", [P, 1])
        prm_rows = sb("prm_rows", [R_END, DEPTH, P])
        prm_all = sb("prm_all", [P, DEPTH, R_END])
        prm = sb("prm", [P, R_END])
        dt_all = sb("dt_all", [P, DEPTH, DN_HEADS])
        al_all = sb("al_all", [P, DEPTH, DN_HEADS])
        pos_i = sb("pos_i", [P, HALVES], I32)
        pos_f = sb("pos_f", [P, HALVES])
        trig = sb("trig", [P, 2, HALVES, ATT_DIM])
        sind, cosd = trig[:, 0, :, :], trig[:, 1, :, :]
        diag = sb("diag", [P, HALVES, P])

        QK = sb("QK", [P, DN_HEADS, 2, SEQ])
        VT = sb("VT", [P, DN_HEADS, SEQ])
        SZ = sb("SZ", [P, DN_HEADS, SEQ])
        early = sb("early", [P, 10 * 256])
        sq = early[:, 0:1536].rearrange("p (b t) -> p b t", b=3)
        inv = early[:, 1536:2560].rearrange("p (b t) -> p b t", b=2)

        def inv_of(h):
            return inv[:, h, :] if h < 2 else sq[:, h - 1, :]

        V = early[:, 0:1024].rearrange("p (u d) -> p u d", u=UNITS)
        Kn = early[:, 1024:1536].rearrange("p (h d) -> p h d", h=DN_HEADS)
        Vd = early[:, 1536:2048].rearrange("p (h d) -> p h d", h=DN_HEADS)
        St = early[:, 2048:2560].rearrange("p (h d) -> p h d", h=DN_HEADS)
        ang = early[:, 0:6 * SEQ].rearrange("p (n t) -> p n t", n=6)
        big = sb("big", [P, HALVES, D_MODEL])
        dec = sb("dec", [P, UNITS, P])
        grow = sb("grow", [P, UNITS, P])
        LT = sb("LT", [P, UNITS, P])
        aT = sb("aT", [P, UNITS, P])
        Dm = sb("Dm", [P, UNITS, P])
        DT = sb("DT", [P, UNITS, P])
        PM = sb("PM", [P, UNITS, P])
        qkr = sb("qkr", [P, HALVES, 512])
        rtmp = VT[:, :, :].rearrange("p (c a) t -> p c (a t)", c=HALVES)
        qT = sb("qT", [P, 2, SEQ])
        kT = sb("kT", [P, 2, SEQ])
        pr = sb("pr", [P, 2, 3 * P])
        prT = sb("prT", [P, 2, 3 * P])
        pooled = sb("pooled", [P, 2, SEQ])
        pw = sb("pw", [P, DEPTH, 2, POOL_DIM])
        pwl = sb("pwl", [P, 2, POOL_DIM])
        mx = sb("mx", [P, ATT_HEADS, 2])
        sm = sb("sm", [P, ATT_HEADS, 2])
        rc = sb("rc", [P, ATT_HEADS, 2])
        ost = sb("ost", [P, HALVES, 8, DN_HEADS])
        ga = sb("ga", [P, 20, 16])
        O, Vn = grow, LT
        Dsq = qkr[:, 0, :]
        R1, QS = Dm[:, 0:4, :], Dm[:, 4:8, :]
        Yf = PM
        squares = [t[:, :, :].rearrange("p a t -> p (a t)") for t in (gact, hid)]

        bank = [ctx.enter_context(nc.psum_tensor(f"bank{i}", [P, NW], F32)) for i in range(8)]
        acc = [[bank[0], bank[1]], [bank[2], bank[3]]]
        gbank, ubank = [bank[4], bank[6]], [bank[5], bank[7]]
        tbank = [bank[4], bank[5], bank[6], bank[7]]

        ident = cst[:, C_IDENT:C_IDENT + P]
        tri = cst[:, C_TRI:C_TRI + P]
        neg = cst[:, C_NEG:C_NEG + P]
        ones = cst[:, C_ONES:C_ONES + P]
        att_mask = cst[:, C_ATT:C_ATT + 3 * P]

        consts_in = signal("consts_in")
        x_in = [signal(f"x_in{c}") for c in range(HALVES)]
        masks_in = signal("masks_in")
        rows_in = signal("rows_in")
        small_in = signal("small_in")
        zeroed = signal("zeroed")
        prm_turned = signal("prm_turned")
        pos_in = signal("pos_in")
        trig_step = signal("trig_step")
        out_ready = signal("out_ready")
        out_written = signal("out_written")
        landed = [signal(f"landed{s}", 16 * SLOT_USES[s]) for s in range(SLOTS)]
        hi_cast = signal("hi_cast", LAYER_PIECES)
        lo_cast = signal("lo_cast", LAYER_PIECES, SLOTS)
        out_used = signal("out_used", OUT_PIECES)
        norm_w_in = signal("norm_w_in", 16 * 3)
        x_new = signal("x_new", 12)
        ss_done = signal("ss_done", 12)
        var_done = signal("var_done", 6)
        ln_done = signal("ln_done", 6)
        rs_done = signal("rs_done", 6)
        newton = signal("newton", 12)
        diag_done = signal("diag_done", 6)
        xw_pool = signal("xw_pool", 9)
        xw_dve = signal("xw_dve", 3)
        turned = signal("turned", 12, 4)
        xh_done = signal("xh_done", 12)
        xl_done = signal("xl_done", 12)
        gates_done = signal("gates_done", 2 * TILES, 2)
        ups_done = signal("ups_done", 2 * TILES, 2)
        downs_done = signal("downs_done", 2 * TILES, 2)
        silu_done = signal("silu_done", 2 * TILES, 2)
        mul_done = signal("mul_done", 2 * TILES, 2)
        ah_done = signal("ah_done", 2 * TILES, 2)
        al_done = signal("al_done", 2 * TILES, 2)
        acc_half = signal("acc_half", 3)
        prm_set = signal("prm_set", 1)
        proj = signal("proj", 16)
        conv1 = signal("conv1", 12)
        conv_mid = signal("conv_mid", 24)
        convd = signal("convd", 12)
        conv_act = signal("conv_act", 12)
        z_act = signal("z_act", 4)
        squared = signal("squared", 4)
        sumsq = signal("sumsq", 4)
        ln2 = signal("ln2", 4)
        inv_done = signal("inv_done", 4)
        normed = signal("normed", 4)
        gates_in = signal("gates_in", 1)
        gstep = signal("gstep", 16)
        gexp = signal("gexp", 1)
        gln = signal("gln", 1)
        tri_g = signal("tri_g", 1)
        cum_col = signal("cum_col", 1)
        cum_row = signal("cum_row", 2)
        cum_read = signal("cum_read", 1)
        eg_done = signal("eg_done", 1)
        neg_eg = signal("neg_eg", 1)
        diff_done = signal("diff_done", 2)
        decayed = signal("decayed", 2)
        gram = signal("gram", 4)
        lt_raw = signal("lt_raw", 4)
        lt_seen = signal("lt_seen", 2)
        at_done = signal("at_done", 4)
        lt_done = signal("lt_done", 2)
        dt0_done = signal("dt0_done", 2)
        d0_turned = signal("d0_turned", 2)
        d_done = signal("d_done", 2 * len(LEVELS))
        p_done = signal("p_done", 2 * len(LEVELS))
        pm_done = signal("pm_done", 2 * len(LEVELS))
        dd_done = signal("dd_done", 2 * len(LEVELS))
        dt_done = signal("dt_done", 2 * len(LEVELS))
        v_turned = signal("v_turned", 2)
        v_copied = signal("v_copied", 2)
        k_turned = signal("k_turned", 1)
        k_copied = signal("k_copied", 1)
        vn_ps = signal("vn_ps", 2)
        vn_done = signal("vn_done", 2)
        vd_done = signal("vd_done", 1)
        st_ps = signal("st_ps", 1)
        st_done = signal("st_done", 1)
        ks_ps = signal("ks_ps", 1)
        qs_ps = signal("qs_ps", 1)
        r1_done = signal("r1_done", 1)
        qs_done = signal("qs_done", 1)
        o_ps = signal("o_ps", 2)
        o_done = signal("o_done", 2)
        o_sq = signal("o_sq", 2)
        o_ss = signal("o_ss", 2)
        o_var = signal("o_var", 2)
        o_ln = signal("o_ln", 2)
        o_rs = signal("o_rs", 2)
        o_newton = signal("o_newton", 6)
        o_newton2 = signal("o_newton2", 2)
        o_normed = signal("o_normed", 2)
        o_turned = signal("o_turned", 2)
        y_gated = signal("y_gated", 2)
        y_hi = signal("y_hi", 2)
        y_lo = signal("y_lo", 2)
        att_in = signal("att_in", 6)
        att_read = signal("att_read", 6)
        rope_cos = signal("rope_cos", 2)
        rope_sin = signal("rope_sin", 2)
        roped = signal("roped", 4)
        qk_turned = signal("qk_turned", 2)
        qk_copied = signal("qk_copied", 2)
        scored = signal("scored", 4)
        masked = signal("masked", 4)
        maxed = signal("maxed", 4)
        exped = signal("exped", 8)
        recip = signal("recip", 4)
        weighted = signal("weighted", 4)
        pr_turned = signal("pr_turned", 4)
        pr_copied = signal("pr_copied", 4)
        att_out = signal("att_out", 2)
        att_hi = signal("att_hi", 2)
        att_lo = signal("att_lo", 2)
        pool_ps = signal("pool_ps", 2)
        pool_copied = signal("pool_copied", 2)
        pool_out = signal("pool_out", 2)
        pool_hi = signal("pool_hi", 2)
        pool_lo = signal("pool_lo", 2)

        FFN = ((ffn1_w_gate, ffn1_w_up, ffn1_w_down), (ffn2_w_gate, ffn2_w_up, ffn2_w_down))

        def cols(ap, layer, first, width=P):
            return ap[layer, :, bass.ds(first, width)].rearrange("(k p) c -> p k c", p=P)

        def piece(t, s):
            return t[:, s, :].rearrange("p (k c) -> p k c", k=KT)

        block = ctx.enter_context(nc.Block())

        @block.sync
        def _(sp):
            for c in range(HALVES):
                sp.dma_start(xr[:, c, :], x[0, c * P:(c + 1) * P, :]).then_inc(x_in[c].sem, 16)
            sp.dma_start(cst[:, 0:C_FIRST], consts[:, 0:C_FIRST]).then_inc(consts_in.sem, 16)

            def load_norm(layer, n, src):
                sp.wait_ge(*turned.at(layer, 4 * n))
                sp.dma_start(norm_w[:, :], src.partition_broadcast(P)).then_inc(norm_w_in.sem, 16)

            def load(layer, index, s, src, dst):
                sp.wait_ge(*lo_cast.at(layer, index - SLOTS + 1))
                sp.dma_start(dst, src).then_inc(landed[s].sem, 16)

            def load_tile(layer, f, t, par):
                gate, up, down = FFN[f]
                base = FFN_BASE[f]
                s = 3 * par
                load(layer, t * 3 + base, s, cols(gate, layer, t * P), piece(raw, s))
                load(layer, t * 3 + (base + 1), s + 1, cols(up, layer, t * P), piece(raw, s + 1))
                load(layer, t * 3 + (base + 2), s + 2, down[layer, bass.ds(t * P, P), :], raw[:, s + 2, :])

            def load_ffn(layer, f):
                if f == 1:
                    gate, up, down = FFN[f]
                    for t in range(2):
                        srcs = (cols(gate, layer, t * P), cols(up, layer, t * P), down[layer, t * P:(t + 1) * P, :])
                        for j in range(3):
                            s = 3 * t + j
                            last = max(i for i in range(MIX_PIECES) if MIX_SLOTS[i] == s)
                            sp.wait_ge(*lo_cast.at(layer, MIX_BASE + last + 1))
                            sp.dma_start(raw[:, s, :] if j == 2 else piece(raw, s), srcs[j]).then_inc(landed[s].sem, 16)
                    with sp.Fori(1, TILES // 2) as g:
                        load_tile(layer, f, g * 2, 0)
                        load_tile(layer, f, g * 2 + 1, 1)
                else:
                    with sp.Fori(0, TILES // 2) as g:
                        load_tile(layer, f, g * 2, 0)
                        load_tile(layer, f, g * 2 + 1, 1)

            with sp.Fori(0, DEPTH) as layer:
                load_norm(layer, 0, ffn1_norm[bass.ds(layer, 1), :].squeeze(0))
                load_ffn(layer, 0)
                load_norm(layer, 1, mix_norm[bass.ds(layer, 1), :].squeeze(0))
                order, covered = list(range(MIX_PIECES)), (FIRST_ATT, FIRST_OUT + OUT_ORDER.index(0))
                for i in covered:
                    order[i:i + 2] = [i + 1, i]
                for i in order:
                    s, q = MIX_SLOTS[i], mix_occupant(i)
                    if i not in covered:
                        sp.wait_ge(*lo_cast.at(layer, MIX_BASE + q + 1 if q >= 0
                                               else FFN_BASE[0] + FFN_PIECES - SLOTS + s + 1))
                    if i < FIRST_ATT:
                        kind, h, j = IN_PIECES[i]
                        first = {"qk": (COL_DQ, COL_DK)[j] + h * P, "gates": IN_WIDTH - P,
                                 "v": COL_DV + h * P, "z": COL_DZ + h * P}[kind]
                        src, dst = cols(w_in, layer, first), piece(raw, s)
                    elif i < FIRST_OUT:
                        src, dst = cols(w_in, layer, COL_AQ + (i - FIRST_ATT) * P), piece(raw, s)
                    else:
                        k = OUT_ORDER[i - FIRST_OUT]
                        src, dst = w_out[layer, k * P:(k + 1) * P, :], raw[:, s, :]
                    sp.dma_start(dst, src).then_inc(landed[s].sem, 16)
                load_norm(layer, 2, ffn2_norm[bass.ds(layer, 1), :].squeeze(0))
                load_ffn(layer, 1)

            load_norm(DEPTH, 0, final_norm)
            sp.wait_ge(out_ready.sem, 1)
            sp.dma_start(out[0, 0:P, :], big[:, 0, :]).then_inc(out_written.sem, 16)
            sp.wait_ge(out_ready.sem, 2)
            sp.dma_start(out[0, P:SEQ, :], big[:, 1, :]).then_inc(out_written.sem, 16)
            sp.wait_ge(out_written.sem, 32)

        @block.gpsimd
        def _(pool):
            one = pool.to_reg(1.0)

            def weigh_rows(layer, n):
                for i in range(3):
                    c, b = divmod(i, 2)
                    q = slice(b * NW, (b + 1) * NW)
                    pool.wait_ge(*norm_w_in.at(layer, 16 * (n + 1)))
                    pool.wait_ge(*x_new.at(layer, 4 * n + i + 1))
                    nc.gpsimd.tensor_tensor(big[:, c, q], xr[:, c, q], norm_w[:, q], ALU.mult).then_inc(xw_pool.sem, 1)

            pool.dma_start(dt_all[:, :, :].rearrange("p l h -> p (l h)"),
                          dn_dt_bias.rearrange("l h -> (l h)").partition_broadcast(P)).then_inc(small_in.sem, 16)
            pool.dma_start(al_all[:, :, :].rearrange("p l h -> p (l h)"),
                          dn_a_log.rearrange("l h -> (l h)").partition_broadcast(P)).then_inc(small_in.sem, 16)
            for l in range(DEPTH):
                for a in range(2):
                    pool.dma_start(pw[a * POOL_DIM:(a + 1) * POOL_DIM, l, :, :],
                                  pool_w[l].rearrange("(j a) c d -> a c j d", a=2)[a]).then_inc(small_in.sem, 16)
            pool.dma_start(cst[:, C_FIRST:], consts[:, C_FIRST:]).then_inc(masks_in.sem, 16)
            weigh_rows(0, 0)
            n_step = [0]

            def step(op):
                n_step[0] += 1
                op.then_inc(trig_step.sem, 1)
                pool.wait_ge(trig_step.sem, n_step[0])

            both = ang[:, 0, :]
            turns, tmp, square, poly = ang[:, 1, :], ang[:, 2, :], ang[:, 3, :], ang[:, 4, :]
            pool.wait_ge(pos_in.sem, 16)
            pool.wait_ge(consts_in.sem, 16)
            step(nc.gpsimd.tensor_copy(pos_f[:, :], pos_i[:, :]))
            half = ATT_DIM // 2
            freq = cst[:, C_FREQ:C_FREQ + half].unsqueeze(1).broadcast_to([P, 2, half])
            for i in range(2):
                for c in range(HALVES):
                    th = both[:, (2 * i + c) * ATT_DIM:(2 * i + c + 1) * ATT_DIM].rearrange("p (a e) -> p a e", a=2)
                    step(nc.gpsimd.tensor_scalar(th, freq, pos_f[:, c:c + 1], None, ALU.mult))
            parts = [3.140625, 0.0, 0.0]
            parts[1] = float(np.round((np.pi - parts[0]) * 2 ** 21) / 2 ** 21)
            parts[2] = np.pi - parts[0] - parts[1]
            rounder = 1.5 * 2 ** 23
            for i, quarter in enumerate((0.0, 0.5)):
                h = slice(i * SEQ // 2, (i + 1) * SEQ // 2)
                step(nc.gpsimd.tensor_scalar(turns[:, h], both[:, h], 1.0 / np.pi, quarter, ALU.mult, ALU.add))
            step(nc.gpsimd.tensor_scalar(turns, turns, rounder, None, ALU.add))
            step(nc.gpsimd.tensor_scalar(turns, turns, -rounder, None, ALU.add))
            for part in parts:
                step(nc.gpsimd.tensor_scalar(tmp, turns, -part, None, ALU.mult))
                step(nc.gpsimd.tensor_tensor(both, both, tmp, ALU.add))
            step(nc.gpsimd.tensor_scalar(both[:, SEQ // 2:], both[:, SEQ // 2:], np.pi / 2, None, ALU.add))
            step(nc.gpsimd.tensor_scalar(tmp, turns, 0.5, rounder, ALU.mult, ALU.add))
            step(nc.gpsimd.tensor_scalar(tmp, tmp, -rounder, -2.0, ALU.add, ALU.mult))
            step(nc.gpsimd.tensor_tensor(turns, turns, tmp, ALU.add))
            step(nc.gpsimd.tensor_tensor(turns, turns, turns, ALU.mult))
            step(nc.gpsimd.tensor_scalar(turns, turns, -2.0, 1.0, ALU.mult, ALU.add))
            step(nc.gpsimd.tensor_tensor(square, both, both, ALU.mult))
            series = [(-1.0) ** k / math.factorial(2 * k + 1) for k in range(8)]
            step(nc.gpsimd.tensor_scalar(poly, square, series[7], series[6], ALU.mult, ALU.add))
            for k in range(5, 0, -1):
                step(nc.gpsimd.tensor_tensor(poly, poly, square, ALU.mult))
                step(nc.gpsimd.tensor_scalar(poly, poly, series[k], None, ALU.add))
            step(nc.gpsimd.tensor_tensor(poly, poly, square, ALU.mult))
            step(nc.gpsimd.tensor_tensor(poly, poly, both, ALU.mult))
            step(nc.gpsimd.tensor_tensor(poly, poly, both, ALU.add))
            step(nc.gpsimd.tensor_tensor(trig[:, :, :, :].rearrange("p i c e -> p (i c e)"), poly, turns, ALU.mult))

            with pool.Fori(0, DEPTH) as layer:
                weigh_rows(layer, 1)
                for c in range(HALVES):
                    pool.wait_ge(*lt_raw.at(layer, 2 * c + 2))
                    pool.sem_inc(lt_seen.sem, 1)
                    u = LT[:, 4 * c:4 * c + 4, :]
                    nc.gpsimd.affine_select(out=u, in_=u, compare_op=ALU.not_equal, fill=one, base=0,
                                            pattern=[[0, 4], [-1, P]],
                                            channel_multiplier=1).then_inc(lt_done.sem, 1)
                for c in range(HALVES):
                    pool.wait_ge(*att_read.at(layer, 2 + c + 1))
                    a8 = big[:, c, 0:512].rearrange("p (h e) -> p h e", e=ATT_DIM)
                    o8 = qkr[:, c, :].rearrange("p (h e) -> p h e", e=ATT_DIM)
                    t8 = rtmp[:, c, :].rearrange("p (h e) -> p h e", e=ATT_DIM)
                    cb = cosd[:, c, :].unsqueeze(1).broadcast_to([P, 8, ATT_DIM])
                    sbd = sind[:, c, :].unsqueeze(1).broadcast_to([P, 8, ATT_DIM])
                    nc.gpsimd.tensor_tensor(o8, a8, cb, ALU.mult).then_inc(rope_cos.sem, 1)
                    nc.gpsimd.tensor_tensor(t8, a8, sbd, ALU.mult).then_inc(rope_sin.sem, 1)
                    pool.wait_ge(*rope_cos.at(layer, c + 1))
                    pool.wait_ge(*rope_sin.at(layer, c + 1))
                    h = ATT_DIM // 2
                    nc.gpsimd.tensor_tensor(o8[:, :, 0:h], o8[:, :, 0:h], t8[:, :, h:],
                                            ALU.subtract).then_inc(roped.sem, 1)
                    nc.gpsimd.tensor_tensor(o8[:, :, h:], o8[:, :, h:], t8[:, :, 0:h],
                                            ALU.add).then_inc(roped.sem, 1)
                weigh_rows(layer, 2)
                weigh_rows(layer, 3)

        @block.tensor
        def _(pe):
            for s, n in ((gates_done, 2), (ups_done, 2), (downs_done, 2), (turned, 4)):
                pe.sem_inc(s.sem, n)
            pe.wait_ge(consts_in.sem, 16)
            pe.wait_ge(rows_in.sem, 16 * 3)
            for l in range(DEPTH):
                nc.tensor.transpose(bank[0][:, l * P:l * P + R_END], prm_rows[:, l, :],
                                    cst[0:R_END, C_IDENT:C_IDENT + R_END]).then_inc(prm_turned.sem, 1)

            def three(outp, lh, ll, rh, rl, start, stop):
                nc.tensor.matmul(outp, lh, rh, start=start, stop=False)
                nc.tensor.matmul(outp, lh, rl, start=False, stop=False)
                return nc.tensor.matmul(outp, ll, rh, start=False, stop=stop)

            def turn_rows(layer, n):
                for c in range(HALVES):
                    pe.wait_ge(*diag_done.at(layer, 2 * n + c + 1))
                    for b in range(2):
                        if c == 1 and b == 1:
                            pe.wait_ge(*xw_dve.at(layer, n + 1))
                        else:
                            pe.wait_ge(*xw_pool.at(layer, 3 * n + 2 * c + b + 1))
                        for k in range(4):
                            m = nc.tensor.matmul(tbank[2 * c + b][:, k * P:(k + 1) * P],
                                                 big[:, c, (4 * b + k) * P:(4 * b + k + 1) * P], diag[:, c, :],
                                                 start=True, stop=True)
                        m.then_inc(turned.sem, 1)

            def column_piece(outp, s, inputs=None):
                for k in range(KT):
                    if inputs is not None and k % (KT // 2) == 0:
                        inputs(k // (KT // 2))
                    m = three(outp, piece(Wh, s)[:, k, :], piece(Wl, s)[:, k, :], Xh[:, k, :], Xl[:, k, :],
                              k == 0, k == KT - 1)
                return m

            def inputs_of(layer, n):
                return lambda half: pe.wait_ge(*xl_done.at(layer, 4 * n + 3 + half))

            def gate_up(layer, f, t, par, inputs=None):
                T = t + f * TILES
                pe.wait_ge(*lo_cast.at(layer, t * 3 + (FFN_BASE[f] + 1)))
                pe.wait_ge(*silu_done.at(layer, T - 1))
                column_piece(gbank[par][:, 0:SEQ], 3 * par, inputs).then_inc(gates_done.sem, 1)
                pe.wait_ge(*lo_cast.at(layer, t * 3 + (FFN_BASE[f] + 2)))
                pe.wait_ge(*mul_done.at(layer, T - 1))
                column_piece(ubank[par][:, 0:SEQ], 3 * par + 1).then_inc(ups_done.sem, 1)

            def down(layer, f, t, par, first=False, last=False):
                T = t + f * TILES
                pe.wait_ge(*lo_cast.at(layer, t * 3 + (FFN_BASE[f] + 3)))
                pe.wait_ge(*al_done.at(layer, T + 1))
                s = 3 * par + 2
                for c in range(HALVES):
                    for n in range(2):
                        m = three(acc[c][n][:, :], aH[:, par, c * P:(c + 1) * P], aL[:, par, c * P:(c + 1) * P],
                                  Wh[:, s, n * NW:(n + 1) * NW], Wl[:, s, n * NW:(n + 1) * NW], first, last)
                    if last and c == 0:
                        m.then_inc(acc_half.sem, 1)
                m.then_inc(downs_done.sem, 1)

            def ffn(layer, f):
                gate_up(layer, f, 0, 0, inputs_of(layer, 2 * f))
                gate_up(layer, f, 1, 1)
                down(layer, f, 0, 0, first=True)
                with pe.Fori(0, TILES // 2 - 1) as g:
                    gate_up(layer, f, g * 2 + 2, 0)
                    down(layer, f, g * 2 + 1, 1)
                    gate_up(layer, f, g * 2 + 3, 1)
                    down(layer, f, g * 2 + 2, 0)
                down(layer, f, TILES - 1, 1, last=True)

            def mixer(layer):
                def split(i):
                    pe.wait_ge(*lo_cast.at(layer, MIX_BASE + i + 1))

                pe.wait_ge(masks_in.sem, 16)
                for i in range(8):
                    split(i)
                    column_piece(bank[i][:, 0:SEQ], MIX_SLOTS[i],
                                 inputs_of(layer, 1) if i == 0 else None).then_inc(proj.sem, 1)
                split(8)
                pe.wait_ge(*convd.at(layer, 1))
                for c in range(HALVES):
                    for k in range(KT):
                        w = slice(P - GATES, P)
                        m = three(bank[0][:, c * GATES:(c + 1) * GATES], Xh[:, k, c * P:(c + 1) * P],
                                  Xl[:, k, c * P:(c + 1) * P], piece(Wh, MIX_SLOTS[8])[:, k, w],
                                  piece(Wl, MIX_SLOTS[8])[:, k, w], k == 0, k == KT - 1)
                m.then_inc(gates_in.sem, 1)
                for h in range(2):
                    split(9 + h)
                    pe.wait_ge(*convd.at(layer, 2 + h))
                    column_piece(bank[1 + h][:, 0:SEQ], MIX_SLOTS[9 + h]).then_inc(proj.sem, 1)
                for h in range(DN_HEADS):
                    pe.wait_ge(*squared.at(layer, h + 1))
                    pe.wait_ge(*convd.at(layer, 4 + h))
                    nc.tensor.matmul(bank[3 + h][:, :], ones, sq[:, h % 3, :], start=True,
                                     stop=True).then_inc(sumsq.sem, 1)
                for h in (2, 3):
                    split(9 + h)
                    if h == 2:
                        pe.wait_ge(*convd.at(layer, 8))
                    else:
                        pe.wait_ge(*gstep.at(layer, 1))
                    column_piece(bank[(5 + h) % 8][:, 0:SEQ], MIX_SLOTS[9 + h]).then_inc(proj.sem, 1)
                pe.wait_ge(*gstep.at(layer, 16))
                pe.wait_ge(*convd.at(layer, 9))
                nc.tensor.matmul(bank[1][:, 0:UNITS], tri, ga[:, 9, 0:UNITS], start=True,
                                 stop=True).then_inc(cum_col.sem, 1)
                pe.wait_ge(*tri_g.at(layer, 1))
                pe.wait_ge(*convd.at(layer, 10))
                pe.wait_ge(*ln2.at(layer, 1))
                for c in range(HALVES):
                    nc.tensor.matmul(bank[2 + c][:, :], ones, grow[:, 4 * c:4 * c + 4, :], start=True,
                                     stop=True).then_inc(cum_row.sem, 1)
                for h in range(2):
                    split(13 + h)
                    pe.wait_ge(*ln2.at(layer, 2 + h))
                    column_piece(bank[4 + h][:, 0:SEQ], MIX_SLOTS[13 + h]).then_inc(proj.sem, 1)
                for n in range(4):
                    b = bank[(6, 7, 0, 1)[n]]
                    if n == 0:
                        pe.wait_ge(*normed.at(layer, 4))
                        pe.wait_ge(*ln2.at(layer, 4))
                    if n == 1:
                        pe.wait_ge(*convd.at(layer, 11))
                    if n == 2:
                        pe.wait_ge(*convd.at(layer, 12))
                    if n == 3:
                        pe.wait_ge(*cum_read.at(layer, 1))
                    for j in range(2):
                        c, h = divmod(2 * n + j, DN_HEADS)
                        t = slice(c * P, (c + 1) * P)
                        m = nc.tensor.matmul(b[:, j * SEQ:(j + 1) * SEQ].rearrange("p (a t) -> p a t", a=2),
                                             QK[:, h, 1, t], QK[:, h, :, t], start=True, stop=True)
                    m.then_inc(gram.sem, 1)
                for h in (2, 3):
                    split(13 + h)
                    pe.wait_ge(*diff_done.at(layer, h - 1))
                    column_piece(bank[h][:, 0:SEQ], MIX_SLOTS[13 + h]).then_inc(proj.sem, 1)
                for c in range(HALVES):
                    pe.wait_ge(*dt0_done.at(layer, c + 1))
                    pe.wait_ge(*z_act.at(layer, c + 1))
                    for h in range(DN_HEADS):
                        m = nc.tensor.transpose(bank[4 + c][:, h * P:(h + 1) * P], DT[:, 4 * c + h, :], ident)
                    m.then_inc(d0_turned.sem, 1)
                for c in range(HALVES):
                    pe.wait_ge(*conv_act.at(layer, 12))
                    pe.wait_ge(*at_done.at(layer, c + 1))
                    for h in range(DN_HEADS):
                        m = nc.tensor.transpose(bank[6 + c][:, h * P:(h + 1) * P], VT[:, h, c * P:(c + 1) * P], ident)
                    m.then_inc(v_turned.sem, 1)
                pe.wait_ge(*at_done.at(layer, 3))
                for h in range(DN_HEADS):
                    m = nc.tensor.transpose(bank[0][:, h * P:(h + 1) * P], QK[:, h, 1, 0:P], ident)
                m.then_inc(k_turned.sem, 1)
                abank = [bank[2], bank[3], bank[1], bank[0], bank[2], bank[3]]

                def att_half(g, c):
                    first, n = ATT_GROUPS[g]
                    split(FIRST_ATT + first + n - 1)
                    s0 = MIX_SLOTS[FIRST_ATT + first]
                    j = 2 * g + c
                    if j < 2:
                        pe.wait_ge(*z_act.at(layer, 3 + j))
                    elif j == 2:
                        pe.wait_ge(*at_done.at(layer, 4))
                    elif j == 3:
                        pe.wait_ge(*k_copied.at(layer, 1))
                    else:
                        pe.wait_ge(*att_read.at(layer, j - 3))
                    b = abank[j][:, 0:n * P].rearrange("p (s c) -> p s c", s=n)
                    for k in range(KT):
                        rh = Wh[:, s0:s0 + n, k * P:(k + 1) * P]
                        rl = Wl[:, s0:s0 + n, k * P:(k + 1) * P]
                        m = three(b, Xh[:, k, c * P:(c + 1) * P], Xl[:, k, c * P:(c + 1) * P], rh, rl,
                                  k == 0, k == KT - 1)
                    m.then_inc(att_in.sem, 1)

                def turn_qk():
                    pe.wait_ge(*roped.at(layer, 4))
                    for j in range(2):
                        for c in range(HALVES):
                            for pair in range(2):
                                m = nc.tensor.transpose(bank[j][:, pair * SEQ + c * P:pair * SEQ + (c + 1) * P],
                                                        qkr[:, c, j * 256 + pair * P:j * 256 + (pair + 1) * P], ident)
                        m.then_inc(qk_turned.sem, 1)

                def level_p(n, c):
                    pe.wait_ge(*d_done.at(layer, 2 * n + c + 1))
                    if n == 0:
                        pe.wait_ge(*lt_done.at(layer, c + 1))
                    for h in range(DN_HEADS):
                        u = 4 * c + h
                        m = nc.tensor.matmul(bank[4 + c][:, h * P:(h + 1) * P], LT[:, u, :], Dm[:, u, :],
                                             start=True, stop=True)
                    m.then_inc(p_done.sem, 1)

                def level_d(n, c):
                    s = LEVELS[n]
                    pe.wait_ge(*pm_done.at(layer, 2 * n + c + 1))
                    if n == 0:
                        pe.wait_ge(*v_copied.at(layer, c + 1))
                    else:
                        pe.wait_ge(*dt_done.at(layer, 2 * n + c - 1))
                    b = bank[6 + c]
                    for h in range(DN_HEADS):
                        u = 4 * c + h
                        pm = PM[:, u, :].rearrange("p (n a s) -> p n a s", a=2, s=s)
                        dt = DT[:, u, :].rearrange("p (n a s) -> p n a s", a=2, s=s)
                        if n < len(LEVELS) - 1:
                            nc.tensor.matmul(b[:, h * 64:(h + 1) * 64].rearrange("p (n s) -> p n s", s=s),
                                             DT[:, u, :], pm[:, :, 0, :], start=True, stop=True)
                        m = nc.tensor.matmul(b[:, 256 + h * 64:256 + (h + 1) * 64]
                                             .rearrange("p (n s) -> p n s", s=s),
                                             PM[:, u, :], dt[:, :, 1, :], start=True, stop=True)
                    m.then_inc(dd_done.sem, 1)

                for n in range(len(LEVELS)):
                    for c in range(HALVES):
                        level_p(n, c)
                    if n == len(LEVELS) - 1:
                        turn_qk()
                    for c in range(HALVES):
                        level_d(n, c)
                    att_half(*divmod(n, 2))

                def scores(h):
                    j, r = h // 2, (h % 2) * ATT_DIM
                    b = bank[h % 2]
                    if h >= 2:
                        pe.wait_ge(*masked.at(layer, h - 1))
                    else:
                        pe.wait_ge(*qk_copied.at(layer, 2))
                    nc.tensor.matmul(b[:, 0:P], qT[r:r + ATT_DIM, j, 0:P], kT[r:r + ATT_DIM, j, 0:P],
                                     start=True, stop=True)
                    nc.tensor.matmul(b[:, P:3 * P], qT[r:r + ATT_DIM, j, P:SEQ], kT[r:r + ATT_DIM, j, :],
                                     start=True, stop=True).then_inc(scored.sem, 1)

                def turn_weights(h):
                    pe.wait_ge(*weighted.at(layer, h + 1))
                    if h == 0:
                        pe.wait_ge(*vn_done.at(layer, 2))
                    else:
                        pe.wait_ge(*pr_copied.at(layer, h))
                    for n in range(3):
                        m = nc.tensor.transpose(bank[7][:, n * P:(n + 1) * P], pr[:, h % 2, n * P:(n + 1) * P], ident)
                    m.then_inc(pr_turned.sem, 1)

                def att_values(h):
                    j, r = h // 2, (h % 2) * ATT_DIM
                    pe.wait_ge(*pr_copied.at(layer, h + 1))
                    if h == 0:
                        pe.wait_ge(*o_done.at(layer, 1))
                    if h == 2:
                        pe.wait_ge(*r1_done.at(layer, 1))
                    v = slice(512 + h * ATT_DIM, 512 + (h + 1) * ATT_DIM)
                    ob = bank[4 + j][r:r + ATT_DIM, :]
                    nc.tensor.matmul(ob[:, 0:P], big[:, 0, v], prT[:, h % 2, 0:P], start=True, stop=True)
                    nc.tensor.matmul(ob[:, P:SEQ], big[:, 0, v], prT[:, h % 2, P:2 * P], start=True, stop=False)
                    m = nc.tensor.matmul(ob[:, P:SEQ], big[:, 1, v], prT[:, h % 2, 2 * P:3 * P], start=False, stop=True)
                    if h % 2:
                        m.then_inc(att_out.sem, 1)

                def out_product(pos):
                    i, k = FIRST_OUT + pos, OUT_ORDER[pos]
                    split(i)
                    if k < 2:
                        pe.wait_ge(*att_lo.at(layer, k + 1))
                    if pos == 0:
                        pe.wait_ge(*masked.at(layer, 4))
                        pe.wait_ge(*pool_lo.at(layer, 2))
                    if k == 4:
                        pe.wait_ge(*y_lo.at(layer, 2))
                    s = MIX_SLOTS[i]
                    for c in range(HALVES):
                        for n in range(2):
                            m = three(acc[c][n][:, :], Xh[:, k, c * P:(c + 1) * P], Xl[:, k, c * P:(c + 1) * P],
                                      Wh[:, s, n * NW:(n + 1) * NW], Wl[:, s, n * NW:(n + 1) * NW],
                                      pos == 0, pos == KT - 1)
                        if pos == KT - 1 and c == 0:
                            m.then_inc(acc_half.sem, 1)
                    m.then_inc(out_used.sem, 1)

                pe.wait_ge(*dt_done.at(layer, 2 * len(LEVELS) - 1))
                pe.wait_ge(*pm_done.at(layer, 2 * len(LEVELS)))
                for h in range(DN_HEADS):
                    m = nc.tensor.matmul(bank[4][:, h * P:(h + 1) * P], DT[:, h, :], V[:, h, :], start=True, stop=True)
                m.then_inc(vn_ps.sem, 1)
                scores(0)
                scores(1)
                pe.wait_ge(*dt_done.at(layer, 2 * len(LEVELS)))
                pe.wait_ge(*vd_done.at(layer, 1))
                for h in range(DN_HEADS):
                    m = nc.tensor.matmul(bank[7][:, h * P:(h + 1) * P], Kn[:, h, :], Vd[:, h, :], start=True, stop=True)
                m.then_inc(st_ps.sem, 1)
                pe.wait_ge(*vn_done.at(layer, 1))
                for h in range(DN_HEADS):
                    m = nc.tensor.matmul(bank[4][:, h * P:(h + 1) * P], aT[:, h, :], Vn[:, h, :], start=True, stop=True)
                m.then_inc(o_ps.sem, 1)
                pe.wait_ge(*st_done.at(layer, 1))
                for h in range(DN_HEADS):
                    m = nc.tensor.matmul(bank[5][:, h * P:(h + 1) * P], QK[:, h, 1, P:SEQ], St[:, h, :], start=True, stop=True)
                m.then_inc(ks_ps.sem, 1)
                for h in range(DN_HEADS):
                    m = nc.tensor.matmul(bank[6][:, h * P:(h + 1) * P], QK[:, h, 0, P:SEQ], St[:, h, :], start=True, stop=True)
                m.then_inc(qs_ps.sem, 1)
                pe.wait_ge(*att_read.at(layer, 6))
                for j in range(2):
                    for a in range(2):
                        g = 2 * j + a
                        at = C_POOL + g * (SEQ + P)
                        u = slice(768 + g * POOL_DIM, 768 + (g + 1) * POOL_DIM)
                        ob = bank[2 + j][a * POOL_DIM:(a + 1) * POOL_DIM, :]
                        nc.tensor.matmul(ob[:, 0:SEQ], big[:, 0, u], cst[:, at:at + SEQ], start=True, stop=False,
                                         skip_group_check=True)
                        m = nc.tensor.matmul(ob[:, P:SEQ], big[:, 1, u], cst[:, at + SEQ:at + SEQ + P],
                                             start=False, stop=True, skip_group_check=True)
                    m.then_inc(pool_ps.sem, 1)
                pe.wait_ge(*r1_done.at(layer, 1))
                for h in range(DN_HEADS):
                    m = nc.tensor.matmul(bank[7][:, h * P:(h + 1) * P], DT[:, 4 + h, :], R1[:, h, :], start=True, stop=True)
                m.then_inc(vn_ps.sem, 1)
                scores(2)
                scores(3)
                pe.wait_ge(*pool_copied.at(layer, 2))
                pe.wait_ge(*vn_done.at(layer, 2))
                pe.wait_ge(*qs_done.at(layer, 1))
                for h in range(DN_HEADS):
                    m = nc.tensor.matmul(bank[6][:, h * P:(h + 1) * P], aT[:, 4 + h, :], Vn[:, 4 + h, :], start=True, stop=True)
                m.then_inc(o_ps.sem, 1)
                turn_weights(0)
                for j in range(2):
                    for a in range(2):
                        r = slice(a * POOL_DIM, (a + 1) * POOL_DIM)
                        m = nc.tensor.matmul(bank[2 + j][r, 0:SEQ], pwl[r, j, :], pooled[r, j, :],
                                             start=True, stop=True)
                    m.then_inc(pool_out.sem, 1)
                att_values(0)
                turn_weights(1)
                att_values(1)
                out_product(0)
                turn_weights(2)
                out_product(1)
                att_values(2)
                turn_weights(3)
                out_product(2)
                att_values(3)
                for c in range(HALVES):
                    pe.wait_ge(*o_normed.at(layer, c + 1))
                    if c == 0:
                        pe.wait_ge(*o_done.at(layer, 2))
                    else:
                        pe.wait_ge(*pr_copied.at(layer, 4))
                    for h in range(DN_HEADS):
                        m = nc.tensor.transpose(bank[6 + c][:, h * P:(h + 1) * P], O[:, 4 * c + h, :], ident)
                    m.then_inc(o_turned.sem, 1)
                for pos in range(3, KT):
                    out_product(pos)

            with pe.Fori(0, DEPTH) as layer:
                turn_rows(layer, 0)
                ffn(layer, 0)
                turn_rows(layer, 1)
                mixer(layer)
                turn_rows(layer, 2)
                ffn(layer, 1)

        def landed_use(layer, f, t_use, s):
            before = 0 if f == 0 else SLOT_USES_FFN + SLOT_USES_MIX[s]
            return landed[s].sem, layer * landed[s].per_layer + (t_use * 16) + 16 * (before + 1)

        def mix_free(i):
            q = mix_occupant(i)
            if q < 0:
                tile, part = divmod(MIX_SLOTS[i], 3)
                return (gates_done, ups_done, downs_done)[part], TILES - 1 + tile
            if q == 8:
                return gates_in, 1
            if q < FIRST_ATT:
                return proj, q + 1 if q < 8 else q
            if q < FIRST_OUT:
                return att_in, 2 * [g for g, (a, n) in enumerate(ATT_GROUPS) if a <= q - FIRST_ATT][-1] + 2
            return out_used, q - FIRST_OUT + 1

        def last_out_use(layer, s):
            return out_used.at(layer, max(k for k in range(OUT_PIECES) if MIX_SLOTS[FIRST_OUT + k] == s) + 1)

        @block.scalar
        def _(act):
            def hi(s):
                return nc.scalar.activation(Wh[:, s, :], raw[:, s, :], ACT.Copy).then_inc(hi_cast.sem, 1)

            def hi_mix(layer, i):
                s = MIX_SLOTS[i]
                act.wait_ge(landed[s].sem, layer * landed[s].per_layer
                            + 16 * (SLOT_USES_FFN + MIX_SLOTS[:i].count(s) + 1))
                sig, n = mix_free(i)
                act.wait_ge(*sig.at(layer, n))
                hi(s)

            def hi_first(layer, f, s):
                act.wait_ge(*landed_use(layer, f, 0, s))
                if f == 0:
                    act.wait_ge(*downs_done.at(layer, -1))
                else:
                    act.wait_ge(*last_out_use(layer, s))
                hi(s)

            def norm(layer, n):
                for c in range(HALVES):
                    for b in range(2):
                        if c == 1 and b == 1:
                            inverse(layer, n, 0)
                        act.wait_ge(*x_new.at(layer, 4 * n + 2 * c + b + 1))
                        if c == 1:
                            act.wait_ge(*ss_done.at(layer, 4 * n + b + 1))
                        nc.scalar.activation(squares[b], xr[:, c, b * NW:(b + 1) * NW], ACT.Square, scale=D_MODEL ** -0.5,
                                             accum_out=stat[:, c, b:b + 1]).then_inc(ss_done.sem, 1)
                inverse(layer, n, 1)

            def inverse(layer, n, c):
                act.wait_ge(*var_done.at(layer, 2 * n + c + 1))
                nc.scalar.activation(stat[:, c, 3:4], stat[:, c, 2:3], ACT.Ln).then_inc(ln_done.sem, 1)
                act.wait_ge(*ln_done.at(layer, 2 * n + c + 1))
                nc.scalar.activation(stat[:, c, 4:5], stat[:, c, 3:4], ACT.Exp, scale=-0.5).then_inc(rs_done.sem, 1)

            def split_rows(layer, n):
                for c in range(HALVES):
                    for b in range(2):
                        act.wait_ge(*turned.at(layer, 4 * n + 2 * c + b + 1))
                        nc.scalar.activation(Xh[:, 4 * b:4 * b + 4, c * P:(c + 1) * P],
                                             tbank[2 * c + b][:, :].rearrange("p (k t) -> p k t", k=4),
                                             ACT.Copy).then_inc(xh_done.sem, 1)

            def step(layer, f, t, par, next_use, follow=None):
                T = t + f * TILES
                s = 3 * (1 - par)

                def cast(j, used):
                    if next_use is not None:
                        act.wait_ge(*landed_use(layer, f, next_use, s + j))
                        act.wait_ge(*used.at(layer, T))
                        hi(s + j)
                    elif follow is not None:
                        if j == 0:
                            act.preload_act_table_set(LN_EXP)
                        follow(j)

                act.wait_ge(*gates_done.at(layer, T + 1))
                act.wait_ge(*mul_done.at(layer, T - 1))
                nc.scalar.activation(gact[:, par, :], gbank[par][:, 0:SEQ], ACT.Silu).then_inc(silu_done.sem, 1)
                cast(0, gates_done)
                cast(1, ups_done)
                act.wait_ge(*mul_done.at(layer, T + 1))
                act.wait_ge(*downs_done.at(layer, T - 1))
                nc.scalar.activation(aH[:, par, :], hid[:, par, :], ACT.Copy).then_inc(ah_done.sem, 1)
                cast(2, downs_done)

            def ffn(layer, f, follow):
                with act.Fori(0, TILES // 2 - 1) as g:
                    step(layer, f, g * 2, 0, g)
                    step(layer, f, g * 2 + 1, 1, g + 1)
                step(layer, f, TILES - 2, 0, TILES // 2 - 1)
                step(layer, f, TILES - 1, 1, None, follow)

            def mixer(layer):
                act.wait_ge(*prm_set.at(layer, 1))
                pieces = ([bank[i] for i in range(8)] + [bank[1], bank[2], bank[7], bank[0]])

                def conv_dst(i):
                    return QK[:, i // 2, i % 2, :] if i < 8 else VT[:, i - 8, :]

                def conv_first(i):
                    col = R_CONV + 3 * 3 * DN_HEADS + tap_row(i)
                    act.wait_ge(*proj.at(layer, i + 1))
                    nc.scalar.activation(conv_dst(i), pieces[i][:, 0:SEQ], ACT.Copy,
                                         scale=prm[:, col:col + 1]).then_inc(conv1.sem, 1)

                def conv_silu(i):
                    act.wait_ge(*convd.at(layer, i + 1))
                    nc.scalar.activation(conv_dst(i), conv_dst(i), ACT.Silu).then_inc(conv_act.sem, 1)

                def square(h):
                    act.wait_ge(*conv_act.at(layer, 2 * h + 2))
                    if h >= 3:
                        act.wait_ge(*sumsq.at(layer, h - 2))
                    nc.scalar.activation(sq[:, h % 3, :], QK[:, h, :, :].rearrange("p a t -> p (a t)"),
                                         ACT.Square).then_inc(squared.sem, 1)

                def log_norm(h):
                    act.wait_ge(*sumsq.at(layer, h + 1))
                    nc.scalar.activation(inv_of(h), bank[3 + h][:, :], ACT.Ln,
                                         bias=bias[:, 0:1]).then_inc(ln2.sem, 1)

                def inverse_norm(h):
                    act.wait_ge(*ln2.at(layer, h + 1))
                    nc.scalar.activation(inv_of(h), inv_of(h), ACT.Exp, scale=-0.5).then_inc(inv_done.sem, 1)

                def z_silu(h):
                    act.wait_ge(*proj.at(layer, 13 + h))
                    nc.scalar.activation(SZ[:, h, :], bank[(4, 5, 2, 3)[h]][:, 0:SEQ],
                                         ACT.Silu).then_inc(z_act.sem, 1)

                for i in range(8):
                    hi_mix(layer, i + 3)
                    conv_first(i)
                    if i >= 1:
                        conv_silu(i - 1)
                        if i % 2 == 0:
                            square(i // 2 - 1)
                hi_mix(layer, 11)
                conv_silu(7)
                conv_first(8)
                hi_mix(layer, 12)
                conv_first(9)
                square(3)
                act.preload_act_table_set(LN_EXP)
                act.wait_ge(*gstep.at(layer, 4))
                nc.scalar.activation(ga[:, 19, 0:4], ga[:, 15, 0:4], ACT.Exp)
                nc.scalar.activation(ga[:, 3, :], ga[:, 2, :], ACT.Exp).then_inc(gexp.sem, 1)
                act.wait_ge(*gstep.at(layer, 5))
                nc.scalar.activation(ga[:, 5, 0:8], ga[:, 4, 0:8], ACT.Ln).then_inc(gln.sem, 1)
                for h in range(DN_HEADS):
                    log_norm(h)
                    inverse_norm(h)
                    if h == 0:
                        hi_mix(layer, 13)
                    if h == 1:
                        conv_first(10)
                    if h == 2:
                        hi_mix(layer, 14)
                conv_first(11)
                hi_mix(layer, 15)
                hi_mix(layer, 16)
                act.wait_ge(*cum_read.at(layer, 1))
                nc.scalar.activation(ga[:, 17, 0:8], ga[:, 16, 0:8], ACT.Exp).then_inc(eg_done.sem, 1)
                for c in range(HALVES):
                    act.wait_ge(*diff_done.at(layer, c + 1))
                    nc.scalar.activation(dec[:, 4 * c:4 * c + 4, :], dec[:, 4 * c:4 * c + 4, :],
                                         ACT.Exp).then_inc(decayed.sem, 1)
                act.preload_act_table_set(SILU)
                z_silu(0)
                z_silu(1)
                for i in range(8, 12):
                    conv_silu(i)
                for i in (17, 18, 19):
                    hi_mix(layer, i)
                z_silu(2)
                z_silu(3)
                act.preload_act_table_set(LN_EXP)
                for c in range(HALVES):
                    act.wait_ge(*d0_turned.at(layer, c + 1))
                    nc.scalar.activation(Dm[:, 4 * c:4 * c + 4, :].rearrange("p u d -> p (u d)"), bank[4 + c][:, :],
                                         ACT.Copy).then_inc(d_done.sem, 1)
                for c in range(HALVES):
                    act.wait_ge(*v_turned.at(layer, c + 1))
                    act.wait_ge(*normed.at(layer, 4))
                    nc.scalar.activation(V[:, 4 * c:4 * c + 4, :].rearrange("p u d -> p (u d)"), bank[6 + c][:, :],
                                         ACT.Copy).then_inc(v_copied.sem, 1)
                act.wait_ge(*k_turned.at(layer, 1))
                nc.scalar.activation(Kn.rearrange("p u d -> p (u d)"), bank[0][:, :], ACT.Copy).then_inc(k_copied.sem, 1)

                def copy_half(g, c):
                    first, n = ATT_GROUPS[g]
                    j = 2 * g + c
                    act.wait_ge(*att_in.at(layer, j + 1))
                    nc.scalar.activation(big[:, c, first * P:(first + n) * P],
                                         bank[(2, 3, 1, 0, 2, 3)[j]][:, 0:n * P], ACT.Copy).then_inc(att_read.sem, 1)

                for n, s in enumerate(LEVELS):
                    if n == len(LEVELS) - 1:
                        for j in range(2):
                            act.wait_ge(*qk_turned.at(layer, j + 1))
                            nc.scalar.activation((qT, kT)[j][:, :, :].rearrange("p a t -> p (a t)"), bank[j][:, :],
                                                 ACT.Copy).then_inc(qk_copied.sem, 1)
                    for c in range(HALVES):
                        act.wait_ge(*dd_done.at(layer, 2 * n + c + 1))
                        b = bank[6 + c]
                        d = Dm[:, 4 * c:4 * c + 4, :].rearrange("p u (n a s) -> p u n a s", a=2, s=s)
                        t = DT[:, 4 * c:4 * c + 4, :].rearrange("p u (n a s) -> p u n a s", a=2, s=s)
                        if n < len(LEVELS) - 1:
                            nc.scalar.activation(d[:, :, :, 0, :], b[:, 0:256].rearrange("p (u n s) -> p u n s", u=4, s=s),
                                                 ACT.Copy).then_inc(d_done.sem, 1)
                        nc.scalar.activation(t[:, :, :, 1, :], b[:, 256:512].rearrange("p (u n s) -> p u n s", u=4, s=s),
                                             ACT.Copy).then_inc(dt_done.sem, 1)
                    for i in LEVEL_CASTS[n]:
                        hi_mix(layer, i)
                    copy_half(*divmod(n, 2))

                def exps(h):
                    act.wait_ge(*maxed.at(layer, h + 1))
                    p = pr[:, h % 2, :]
                    nc.scalar.activation(p[:, 0:P], p[:, 0:P], ACT.Exp, bias=mx[:, h, 0:1],
                                         accum_out=sm[:, h, 0:1]).then_inc(exped.sem, 1)
                    nc.scalar.activation(p[:, P:], p[:, P:], ACT.Exp, bias=mx[:, h, 1:2],
                                         accum_out=sm[:, h, 1:2]).then_inc(exped.sem, 1)

                def out_stats(c):
                    act.wait_ge(*o_done.at(layer, c + 1))
                    if c:
                        act.wait_ge(*o_ss.at(layer, 1))
                    nc.scalar.activation(Dsq, O[:, 4 * c:4 * c + 4, :].rearrange("p u d -> p (u d)"),
                                         ACT.Square).then_inc(o_sq.sem, 1)

                def out_inverse(c):
                    act.wait_ge(*o_var.at(layer, c + 1))
                    nc.scalar.activation(ost[:, c, 2, :], ost[:, c, 1, :], ACT.Ln).then_inc(o_ln.sem, 1)
                    act.wait_ge(*o_ln.at(layer, c + 1))
                    nc.scalar.activation(ost[:, c, 3, :], ost[:, c, 2, :], ACT.Exp, scale=-0.5).then_inc(o_rs.sem, 1)

                def copy_weights(h):
                    act.wait_ge(*pr_turned.at(layer, h + 1))
                    nc.scalar.activation(prT[:, h % 2, :], bank[7][:, 0:3 * P], ACT.Copy).then_inc(pr_copied.sem, 1)

                act.wait_ge(*st_ps.at(layer, 1))
                nc.scalar.activation(St.rearrange("p u d -> p (u d)"), bank[7][:, :], ACT.Copy).then_inc(st_done.sem, 1)
                exps(0)
                exps(1)
                act.wait_ge(*o_ps.at(layer, 1))
                nc.scalar.activation(O[:, 0:4, :].rearrange("p u d -> p (u d)"), bank[4][:, :],
                                     ACT.Copy).then_inc(o_done.sem, 1)
                for j in range(2):
                    act.wait_ge(*pool_ps.at(layer, j + 1))
                    nc.scalar.activation(pooled[:, j, :], bank[2 + j][:, 0:SEQ], ACT.Copy).then_inc(pool_copied.sem, 1)
                out_stats(0)
                copy_weights(0)
                for j in range(2):
                    act.wait_ge(*pool_out.at(layer, j + 1))
                    nc.scalar.activation(Xh[:, 2 + j, :], bank[2 + j][:, 0:SEQ], ACT.Copy,
                                         scale=prm[:, R_PSCALE + j:R_PSCALE + j + 1]).then_inc(pool_hi.sem, 1)
                copy_weights(1)
                out_stats(1)
                exps(2)
                exps(3)
                out_inverse(0)
                out_inverse(1)
                act.wait_ge(*att_out.at(layer, 1))
                nc.scalar.activation(Xh[:, 0, :], bank[4][:, 0:SEQ], ACT.Copy).then_inc(att_hi.sem, 1)
                hi_mix(layer, 29)
                copy_weights(2)
                copy_weights(3)
                hi_mix(layer, 30)
                act.wait_ge(*att_out.at(layer, 2))
                nc.scalar.activation(Xh[:, 1, :], bank[5][:, 0:SEQ], ACT.Copy).then_inc(att_hi.sem, 1)
                for c in range(HALVES):
                    act.wait_ge(*y_gated.at(layer, c + 1))
                    nc.scalar.activation(Xh[:, 4:8, c * P:(c + 1) * P], Yf[:, 4 * c:4 * c + 4, :],
                                         ACT.Copy).then_inc(y_hi.sem, 1)
                hi_mix(layer, 31)
                hi_mix(layer, 32)

            act.dma_start(pos_i[:, :], positions[0].rearrange("(c p) -> p c", p=P),
                          allow_slow_non_contiguous=True).then_inc(pos_in.sem, 16)
            act.dma_start(prm_rows[0:R_PSCALE, :, :],
                          dn_conv_w.rearrange("l t (r c) -> (t r) l c", c=P)).then_inc(rows_in.sem, 16)
            act.dma_start(prm_rows[R_PSCALE:R_ONORM, :, :],
                          pool_scale.rearrange("l (r c) -> r l c", c=P)).then_inc(rows_in.sem, 16)
            act.dma_start(prm_rows[R_ONORM:R_END, :, :],
                          dn_out_norm.rearrange("(a l) c -> a l c", a=1)).then_inc(rows_in.sem, 16)

            with act.Fori(0, DEPTH) as layer:
                act.preload_act_table_set(LN_EXP)
                norm(layer, 0)
                hi_first(layer, 0, 0)
                split_rows(layer, 0)
                act.preload_act_table_set(SILU)
                hi_first(layer, 0, 1)
                hi_first(layer, 0, 2)
                ffn(layer, 0, lambda j: hi_mix(layer, j))
                norm(layer, 1)
                split_rows(layer, 1)
                act.preload_act_table_set(SILU)
                mixer(layer)
                for s in range(3):
                    hi_first(layer, 1, s)
                norm(layer, 2)
                split_rows(layer, 2)
                act.preload_act_table_set(SILU)
                ffn(layer, 1, lambda j: None)
            norm(DEPTH, 0)

        @block.vector
        def _(dve):
            def lo(s):
                return nc.vector.tensor_tensor(Wl[:, s, :], raw[:, s, :], Wh[:, s, :].bitcast(F32),
                                               ALU.subtract).then_inc(lo_cast.sem, 1)

            def lo_piece(layer, index, s):
                dve.wait_ge(*hi_cast.at(layer, index + 1))
                lo(s)

            def lo_mix(layer, i):
                lo_piece(layer, MIX_BASE + i, MIX_SLOTS[i])

            def variance(layer, n, c):
                st = [stat[:, c, i:i + 1] for i in range(8)]
                dve.wait_ge(*ss_done.at(layer, 4 * n + 2 * c + 2))
                nc.vector.tensor_scalar(st[2], st[0], st[1], EPS, ALU.add, ALU.add).then_inc(var_done.sem, 1)

            def refine(layer, n, c):
                st = [stat[:, c, i:i + 1] for i in range(8)]
                dve.wait_ge(*rs_done.at(layer, 2 * n + c + 1))
                nc.vector.scalar_tensor_tensor(st[5], st[2], st[4], st[4], ALU.mult, ALU.mult).then_inc(newton.sem, 1)
                dve.wait_ge(*newton.at(layer, 2 * (2 * n + c) + 1))
                nc.vector.tensor_scalar(st[6], st[5], -0.5, 1.5, ALU.mult, ALU.add).then_inc(newton.sem, 1)
                dve.wait_ge(*newton.at(layer, 2 * (2 * n + c) + 2))
                return st[6], st[4]

            def weigh_quarter(layer, n):
                dve.wait_ge(*norm_w_in.at(layer, 16 * (n + 1)))
                nc.vector.tensor_tensor(big[:, 1, NW:], xr[:, 1, NW:], norm_w[:, NW:], ALU.mult).then_inc(xw_dve.sem, 1)

            def norm(layer, n, update_quarter):
                update_quarter(0, 0)
                update_quarter(0, 1)
                update_quarter(1, 0)
                variance(layer, n, 0)
                update_quarter(1, 1)
                for c in range(HALVES):
                    a, b = refine(layer, n, c)
                    nc.vector.tensor_scalar(diag[:, c, :], ident, a, b, ALU.mult, ALU.mult).then_inc(diag_done.sem, 1)
                    if c == 0:
                        variance(layer, n, 1)
                        weigh_quarter(layer, n)

            def split_rows(layer, n):
                for c in range(HALVES):
                    for b in range(2):
                        dve.wait_ge(*xh_done.at(layer, 4 * n + 2 * c + b + 1))
                        t = slice(c * P, (c + 1) * P)
                        nc.vector.tensor_tensor(Xl[:, 4 * b:4 * b + 4, t],
                                                tbank[2 * c + b][:, :].rearrange("p (k t) -> p k t", k=4),
                                                Xh[:, 4 * b:4 * b + 4, t].bitcast(F32), ALU.subtract).then_inc(xl_done.sem, 1)

            def step(layer, f, t, par, cast_next, follow=None):
                T = t + f * TILES
                s = 3 * (1 - par)

                def cast(j):
                    if cast_next:
                        dve.wait_ge(*hi_cast.at(layer, t * 3 + (FFN_BASE[f] + 3 + j + 1)))
                        lo(s + j)
                    elif follow is not None:
                        follow(j)

                cast(0)
                dve.wait_ge(*silu_done.at(layer, T + 1))
                dve.wait_ge(*ups_done.at(layer, T + 1))
                nc.vector.tensor_tensor(hid[:, par, :], ubank[par][:, 0:SEQ], gact[:, par, :],
                                        ALU.mult).then_inc(mul_done.sem, 1)
                cast(1)
                dve.wait_ge(*ah_done.at(layer, T + 1))
                nc.vector.tensor_tensor(aL[:, par, :], hid[:, par, :], aH[:, par, :].bitcast(F32),
                                        ALU.subtract).then_inc(al_done.sem, 1)
                cast(2)

            def ffn(layer, f, follow):
                with dve.Fori(0, TILES // 2 - 1) as g:
                    step(layer, f, g * 2, 0, True)
                    step(layer, f, g * 2 + 1, 1, True)
                step(layer, f, TILES - 2, 0, True)
                step(layer, f, TILES - 1, 1, False, follow)

            def update(layer, part, scale, done):
                def quarter(c, b):
                    if b == 0:
                        if c == 0:
                            dve.wait_ge(*acc_half.at(layer, part + 1))
                        else:
                            dve.wait_ge(*done)
                    r = xr[:, c, b * NW:(b + 1) * NW]
                    nc.vector.scalar_tensor_tensor(r, acc[c][b][:, :], scale, r, ALU.mult, ALU.add).then_inc(x_new.sem, 1)
                return quarter

            def mixer(layer):
                def conv_rest(i):
                    src = ([bank[b] for b in range(8)] + [bank[1], bank[2], bank[7], bank[0]])[i]
                    dst = QK[:, i // 2, i % 2, :] if i < 8 else VT[:, i - 8, :]
                    dve.wait_ge(*conv1.at(layer, i + 1))
                    for back in range(1, TAPS):
                        col = R_CONV + (TAPS - 1 - back) * 3 * DN_HEADS + tap_row(i)
                        op = nc.vector.scalar_tensor_tensor(dst[:, back:], src[:, 0:SEQ - back], prm[:, col:col + 1],
                                                            dst[:, back:], ALU.mult, ALU.add)
                        if back < TAPS - 1:
                            op.then_inc(conv_mid.sem, 1)
                            dve.wait_ge(*conv_mid.at(layer, 2 * i + back))
                        else:
                            op.then_inc(convd.sem, 1)

                count = [0]

                def small(op):
                    count[0] += 1
                    op.then_inc(gstep.sem, 1)
                    dve.wait_ge(*gstep.at(layer, count[0]))

                gin = ga[:, 0, :].rearrange("p (c e) -> p c e", c=2)
                gneg = ga[:, 2, :].rearrange("p (c e) -> p c e", c=2)
                gex = ga[:, 3, :].rearrange("p (c e) -> p c e", c=2)

                def row(n):
                    return ga[:, n, 0:8].rearrange("p (c e) -> p c e", c=2)

                def per_head(n):
                    return ga[:, n, 0:4].unsqueeze(1).broadcast_to([P, 2, 4])

                for i in range(8):
                    lo_mix(layer, i + 3)
                    conv_rest(i)
                lo_mix(layer, 11)
                dve.wait_ge(*gates_in.at(layer, 1))
                small(nc.vector.tensor_copy(ga[:, 0, :], bank[0][:, 0:16]))
                small(nc.vector.tensor_tensor(row(1), gin[:, :, 4:8], per_head(14), ALU.add))
                small(nc.vector.tensor_scalar(gneg[:, :, 0:4], gin[:, :, 0:4], -1.0, 87.0, ALU.mult, ALU.min))
                small(nc.vector.scalar_tensor_tensor(gneg[:, :, 4:8], row(1), -1.0, row(1), ALU.mult, ALU.min))
                conv_rest(8)
                lo_mix(layer, 12)
                dve.wait_ge(*gexp.at(layer, 1))
                e = gex[:, :, 4:8]
                small(nc.vector.tensor_scalar(row(4), e, 1.0, None, ALU.add))
                small(nc.vector.tensor_scalar(row(6), gex[:, :, 0:4], 1.0, None, ALU.add))
                small(nc.vector.reciprocal(ga[:, 7, 0:8], ga[:, 6, 0:8]))
                small(nc.vector.tensor_scalar(row(8), row(4), -1.0, 1e-30, ALU.add, ALU.max))
                small(nc.vector.reciprocal(ga[:, 10, 0:8], ga[:, 8, 0:8]))
                small(nc.vector.tensor_tensor(row(11), row(10), e, ALU.mult))
                small(nc.vector.tensor_scalar(row(12), e, -0.5, 1.0, ALU.mult, ALU.add))
                small(nc.vector.tensor_tensor(row(13), row(12), e, ALU.mult))
                dve.wait_ge(*gln.at(layer, 1))
                small(nc.vector.tensor_tensor(ga[:, 11, 0:8], ga[:, 11, 0:8], ga[:, 5, 0:8], ALU.mult))
                small(nc.vector.tensor_tensor(ga[:, 11, 0:8], ga[:, 11, 0:8], ga[:, 13, 0:8], ALU.max))
                small(nc.vector.scalar_tensor_tensor(ga[:, 1, 0:8], ga[:, 1, 0:8], 0.0, ga[:, 11, 0:8], ALU.max, ALU.add))
                small(nc.vector.scalar_tensor_tensor(row(9), row(1), -1.0, per_head(19), ALU.mult, ALU.mult))
                beta, gc, eg, neg_e = ga[:, 7, :], ga[:, 16, :], ga[:, 17, :], ga[:, 18, :]
                nc.vector.tensor_tensor(grow[:, :, :], tri.unsqueeze(1).broadcast_to([P, UNITS, P]),
                                        ga[:, 9, 0:8].unsqueeze(2).broadcast_to([P, UNITS, P]),
                                        ALU.mult).then_inc(tri_g.sem, 1)
                conv_rest(9)

                def l2norm(h):
                    dve.wait_ge(*inv_done.at(layer, h + 1))
                    q, k = QK[:, h, 0, :], QK[:, h, 1, :]
                    nc.vector.scalar_tensor_tensor(q, q, DN_SCALE, inv_of(h)[:, 0:SEQ], ALU.mult, ALU.mult)
                    nc.vector.tensor_tensor(k, k, inv_of(h)[:, SEQ:], ALU.mult).then_inc(normed.sem, 1)

                l2norm(0)
                lo_mix(layer, 13)
                l2norm(1)
                conv_rest(10)
                l2norm(2)
                lo_mix(layer, 14)
                l2norm(3)
                conv_rest(11)
                dve.wait_ge(*cum_col.at(layer, 1))
                nc.vector.tensor_copy(gc[:, 0:8], bank[1][:, 0:8]).then_inc(cum_read.sem, 1)
                dve.wait_ge(*cum_read.at(layer, 1))
                for c in range(HALVES):
                    dve.wait_ge(*cum_row.at(layer, c + 1))
                    for h in range(DN_HEADS):
                        u = 4 * c + h
                        op = nc.vector.scalar_tensor_tensor(dec[:, u, :], bank[2 + c][:, h * P:(h + 1) * P], gc[:, u:u + 1],
                                                            neg, ALU.subtract, ALU.add)
                    op.then_inc(diff_done.sem, 1)
                lo_mix(layer, 15)
                lo_mix(layer, 16)
                dve.wait_ge(*eg_done.at(layer, 1))
                nc.vector.tensor_scalar(neg_e[:, 0:8], eg[:, 0:8], -1.0, None, ALU.mult).then_inc(neg_eg.sem, 1)

                def unit_gram(n):
                    c = n // 2
                    dve.wait_ge(*gram.at(layer, n + 1))
                    dve.wait_ge(*decayed.at(layer, c + 1))
                    b = bank[(6, 7, 0, 1)[n]][:, :].rearrange("p (u a t) -> p u a t", u=2, a=2)
                    for j in range(2):
                        u = 2 * n + j
                        op = nc.vector.scalar_tensor_tensor(LT[:, u, :], b[:, j, 1, :], beta[:, u:u + 1], dec[:, u, :],
                                                            ALU.mult, ALU.mult)
                    op.then_inc(lt_raw.sem, 1)
                    nc.vector.tensor_tensor(aT[:, 2 * n:2 * n + 2, :], b[:, :, 0, :], dec[:, 2 * n:2 * n + 2, :],
                                            ALU.mult).then_inc(at_done.sem, 1)

                for n in range(4):
                    unit_gram(n)
                for c in range(HALVES):
                    dve.wait_ge(*lt_done.at(layer, c + 1))
                    pair = cst[:, C_PAIR:C_PAIR + P].unsqueeze(1).broadcast_to([P, 4, P])
                    nc.vector.tensor_tensor(DT[:, 4 * c:4 * c + 4, :], LT[:, 4 * c:4 * c + 4, :], pair,
                                            ALU.mult).then_inc(dt0_done.sem, 1)
                for i in (17, 18, 19):
                    lo_mix(layer, i)
                for n in range(len(LEVELS)):
                    mask = cst[:, C_LEVEL + n * P:C_LEVEL + (n + 1) * P].unsqueeze(1).broadcast_to([P, 4, P])
                    for c in range(HALVES):
                        dve.wait_ge(*p_done.at(layer, 2 * n + c + 1))
                        nc.vector.tensor_tensor(PM[:, 4 * c:4 * c + 4, :],
                                                bank[4 + c][:, :].rearrange("p (u t) -> p u t", u=4), mask,
                                                ALU.mult).then_inc(pm_done.sem, 1)
                    for i in LEVEL_CASTS[n]:
                        lo_mix(layer, i)

                def new_values(c):
                    u = slice(4 * c, 4 * c + 4)
                    dve.wait_ge(*vn_ps.at(layer, c + 1))
                    nc.vector.tensor_tensor(Vn[:, u, :], bank[(4, 7)[c]][:, :].rearrange("p (u d) -> p u d", u=4),
                                            beta[:, u].unsqueeze(2).broadcast_to([P, 4, P]), ALU.mult).then_inc(vn_done.sem, 1)

                def mask_scores(h):
                    dve.wait_ge(*scored.at(layer, h + 1))
                    if h >= 2:
                        dve.wait_ge(*pr_turned.at(layer, h - 1))
                    p = pr[:, h % 2, :]
                    nc.vector.scalar_tensor_tensor(p, bank[h % 2][:, 0:3 * P], ATT_SCALE, att_mask, ALU.mult,
                                                   ALU.add).then_inc(masked.sem, 1)
                    dve.wait_ge(*masked.at(layer, h + 1))
                    nc.vector.tensor_reduce(mx[:, h, 0:1], p[:, 0:P], AX.X, ALU.max, negate=True)
                    nc.vector.tensor_reduce(mx[:, h, 1:2], p[:, P:], AX.X, ALU.max, negate=True).then_inc(maxed.sem, 1)

                def weigh(h):
                    dve.wait_ge(*exped.at(layer, 2 * h + 2))
                    nc.vector.reciprocal(rc[:, h, :], sm[:, h, :]).then_inc(recip.sem, 1)
                    dve.wait_ge(*recip.at(layer, h + 1))
                    p = pr[:, h % 2, :]
                    nc.vector.tensor_scalar(p[:, 0:P], p[:, 0:P], rc[:, h, 0:1], None, ALU.mult)
                    nc.vector.tensor_scalar(p[:, P:], p[:, P:], rc[:, h, 1:2], None, ALU.mult).then_inc(weighted.sem, 1)

                def out_variance(c):
                    dve.wait_ge(*o_sq.at(layer, c + 1))
                    nc.vector.tensor_reduce(ost[:, c, 0, :], Dsq.rearrange("p (u d) -> p u d", u=4), AX.X,
                                            ALU.add).then_inc(o_ss.sem, 1)
                    dve.wait_ge(*o_ss.at(layer, c + 1))
                    nc.vector.tensor_scalar(ost[:, c, 1, :], ost[:, c, 0, :], 1.0 / P, EPS, ALU.mult,
                                            ALU.add).then_inc(o_var.sem, 1)

                def out_norm(c):
                    dve.wait_ge(*o_rs.at(layer, c + 1))
                    s = [ost[:, c, i, :] for i in range(8)]
                    nc.vector.tensor_tensor(s[4], s[3], s[3], ALU.mult).then_inc(o_newton.sem, 1)
                    dve.wait_ge(*o_newton.at(layer, 3 * c + 1))
                    nc.vector.tensor_tensor(s[5], s[4], s[1], ALU.mult).then_inc(o_newton.sem, 1)
                    dve.wait_ge(*o_newton.at(layer, 3 * c + 2))
                    nc.vector.tensor_scalar(s[6], s[5], -0.5, 1.5, ALU.mult, ALU.add).then_inc(o_newton.sem, 1)
                    dve.wait_ge(*o_newton.at(layer, 3 * c + 3))
                    nc.vector.tensor_tensor(s[7], s[6], s[3], ALU.mult).then_inc(o_newton2.sem, 1)
                    dve.wait_ge(*o_newton2.at(layer, c + 1))
                    o = O[:, 4 * c:4 * c + 4, :]
                    nc.vector.tensor_tensor(o, o, s[7].unsqueeze(2).broadcast_to([P, 4, P]),
                                            ALU.mult).then_inc(o_normed.sem, 1)

                new_values(0)
                dve.wait_ge(*vn_done.at(layer, 1))
                nc.vector.tensor_tensor(Vd, Vn[:, 0:4, :], dec[:, 0:4, P - 1:P].broadcast_to([P, 4, P]),
                                        ALU.mult).then_inc(vd_done.sem, 1)
                mask_scores(0)
                mask_scores(1)
                dve.wait_ge(*ks_ps.at(layer, 1))
                dve.wait_ge(*neg_eg.at(layer, 1))
                for h in range(DN_HEADS):
                    op = nc.vector.scalar_tensor_tensor(R1[:, h, :], bank[5][:, h * P:(h + 1) * P], neg_e[:, 4 + h:5 + h],
                                                        V[:, 4 + h, :], ALU.mult, ALU.add)
                op.then_inc(r1_done.sem, 1)
                dve.wait_ge(*qs_ps.at(layer, 1))
                nc.vector.tensor_tensor(QS, bank[6][:, :].rearrange("p (u d) -> p u d", u=4),
                                        eg[:, 4:8].unsqueeze(2).broadcast_to([P, 4, P]), ALU.mult).then_inc(qs_done.sem, 1)
                weigh(0)
                weigh(1)
                new_values(1)
                out_variance(0)
                dve.wait_ge(*o_ps.at(layer, 2))
                nc.vector.tensor_tensor(O[:, 4:8, :], bank[6][:, :].rearrange("p (u d) -> p u d", u=4), QS,
                                        ALU.add).then_inc(o_done.sem, 1)
                mask_scores(2)
                for j in range(2):
                    dve.wait_ge(*pool_hi.at(layer, j + 1))
                    nc.vector.scalar_tensor_tensor(Xl[:, 2 + j, :], bank[2 + j][:, 0:SEQ],
                                                   prm[:, R_PSCALE + j:R_PSCALE + j + 1],
                                                   Xh[:, 2 + j, :].bitcast(F32), ALU.mult, ALU.subtract).then_inc(pool_lo.sem, 1)
                mask_scores(3)
                out_variance(1)
                weigh(2)
                weigh(3)
                out_norm(0)
                out_norm(1)
                dve.wait_ge(*att_hi.at(layer, 1))
                nc.vector.tensor_tensor(Xl[:, 0, :], bank[4][:, 0:SEQ], Xh[:, 0, :].bitcast(F32),
                                        ALU.subtract).then_inc(att_lo.sem, 1)
                lo_mix(layer, 29)
                lo_mix(layer, 30)
                dve.wait_ge(*att_hi.at(layer, 2))
                nc.vector.tensor_tensor(Xl[:, 1, :], bank[5][:, 0:SEQ], Xh[:, 1, :].bitcast(F32),
                                        ALU.subtract).then_inc(att_lo.sem, 1)
                for c in range(HALVES):
                    u = slice(4 * c, 4 * c + 4)
                    dve.wait_ge(*o_turned.at(layer, c + 1))
                    nc.vector.scalar_tensor_tensor(Yf[:, u, :], bank[6 + c][:, :].rearrange("p (u d) -> p u d", u=4),
                                                   prm[:, R_ONORM:R_ONORM + 1], SZ[:, :, c * P:(c + 1) * P],
                                                   ALU.mult, ALU.mult).then_inc(y_gated.sem, 1)
                for c in range(HALVES):
                    dve.wait_ge(*y_hi.at(layer, c + 1))
                    nc.vector.tensor_tensor(Xl[:, 4:8, c * P:(c + 1) * P], Yf[:, 4 * c:4 * c + 4, :],
                                            Xh[:, 4:8, c * P:(c + 1) * P].bitcast(F32), ALU.subtract).then_inc(y_lo.sem, 1)
                lo_mix(layer, 31)
                lo_mix(layer, 32)

            for s, n in ((lo_cast, SLOTS), (silu_done, 2), (mul_done, 2), (ah_done, 2), (al_done, 2)):
                dve.sem_inc(s.sem, n)
            nc.vector.memset(bias[:, 0:1], EPS).then_inc(zeroed.sem, 1)
            dve.wait_ge(zeroed.sem, 1)
            dve.wait_ge(consts_in.sem, 16)
            dve.wait_ge(prm_turned.sem, DEPTH)
            nc.vector.tensor_copy(prm_all[:, :, :], bank[0][:, 0:DEPTH * P]
                                  .rearrange("p (l r) -> p l r", l=DEPTH)[:, :, 0:R_END]).then_inc(zeroed.sem, 1)
            dve.wait_ge(zeroed.sem, 2)
            for c in range(HALVES):
                dve.wait_ge(x_in[c].sem, 16)
                dve.sem_inc(x_new.sem, 2)

            def no_update(c, b):
                pass

            with dve.Fori(0, DEPTH) as layer:
                norm(layer, 0, no_update)
                split_rows(layer, 0)
                for s in range(3):
                    lo_piece(layer, s, s)
                ffn(layer, 0, lambda j: lo_mix(layer, j) if j < 2 else None)
                norm(layer, 1, update(layer, 0, 0.5, downs_done.at(layer, TILES)))
                split_rows(layer, 1)
                lo_mix(layer, 2)
                dve.wait_ge(small_in.sem, 16 * (2 * DEPTH + 2))
                dve.wait_ge(masks_in.sem, 16)
                nc.vector.tensor_copy(prm[:, :], prm_all[:, bass.ds(layer, 1), :].squeeze(1))
                nc.vector.tensor_copy(pwl[:, :, :].rearrange("p j d -> p (j d)"),
                                      pw[:, bass.ds(layer, 1), :, :].squeeze(1).rearrange("p j d -> p (j d)"))
                nc.vector.tensor_copy(ga[:, 14, 0:4], dt_all[:, bass.ds(layer, 1), :].squeeze(1))
                nc.vector.tensor_copy(ga[:, 15, 0:4], al_all[:, bass.ds(layer, 1), :].squeeze(1)).then_inc(prm_set.sem, 1)
                dve.wait_ge(*prm_set.at(layer, 1))
                mixer(layer)
                for j in range(3):
                    lo_piece(layer, FFN_BASE[1] + j, j)
                norm(layer, 2, update(layer, 1, 1.0, out_used.at(layer, OUT_PIECES)))
                split_rows(layer, 2)
                ffn(layer, 1, None)
                quarter = update(layer, 2, 0.5, downs_done.at(layer, 2 * TILES))
                for c in range(HALVES):
                    for b in range(2):
                        quarter(c, b)
            variance(DEPTH, 0, 0)
            variance(DEPTH, 0, 1)
            weigh_quarter(DEPTH, 0)
            dve.wait_ge(*xw_dve.at(DEPTH, 1))
            for c in range(HALVES):
                a, b = refine(DEPTH, 0, c)
                dve.wait_ge(*xw_pool.at(DEPTH, 2 + c))
                nc.vector.tensor_scalar(big[:, c, :], big[:, c, :], a, b, ALU.mult, ALU.mult).then_inc(out_ready.sem, 1)


_INS = ("x", "positions", "ffn1_norm", "ffn1_w_gate", "ffn1_w_up", "ffn1_w_down", "mix_norm", "w_in", "pool_w",
        "pool_scale", "dn_conv_w", "dn_a_log", "dn_dt_bias", "dn_out_norm", "w_out", "ffn2_norm", "ffn2_w_gate",
        "ffn2_w_up", "ffn2_w_down", "final_norm")


def kernel(**inputs):
    import concourse.bacc as bacc
    from concourse.bass_utils import run_bass_kernel_spmd

    nc = bacc.Bacc("TRN2", target_bir_lowering=False, num_devices=1)
    arrays = {n: np.ascontiguousarray(inputs[n]) for n in _INS}
    arrays["consts"] = constants()
    args = {n: nc.dram_tensor(f"in_{n}", a.shape, mybir.dt.from_np(a.dtype), kind="ExternalInput").ap()
            for n, a in arrays.items()}
    args["out"] = nc.dram_tensor("out_x", (1, SEQ, D_MODEL), F32, kind="ExternalOutput").ap()
    build(nc, **args)
    r = run_bass_kernel_spmd(nc, [{f"in_{n}": a for n, a in arrays.items()}], core_ids=[0])
    return r.results[0]["out_x"]
```
